# Optimizing a Trainium2 kernel written in Bass

```python
import jax, jax.numpy as jnp
from jax import lax
import numpy as np

"""One inference step of a 2-layer hybrid causal decoder trunk, run for a prompt group and a sample group that share all weights.

Layer 0 (even): parallel head groups A = sliding-window GQA (ALiBi, learned sinks) and B = gated short conv.
Layer 1 (odd): parallel head groups C = multi-scale causal pooling and D = dilated sliding-window attention (ALiBi).
Every layer: DeepNorm post-LN residual x <- LN(alpha*x + mixer(x)); x <- LN(alpha*x + sqrelu_mlp(x)).

Inputs: x_prompt (BATCH, SEQ, D_MODEL); x_sample (DEC_BATCH, DEC_SEQ, D_MODEL);
 cache_a_k / cache_a_v (N_EVEN, DEC_BATCH, min(A_WINDOW, PAST_LEN), A_KV_HEADS, HEAD_DIM)
 state_b_conv (N_EVEN, DEC_BATCH, CONV_WIDTH-1, B_WIDTH)
 state_c_pool (N_ODD, DEC_BATCH, POOL_MAX-1, C_WIDTH)
 cache_d_k / cache_d_v (N_ODD, DEC_BATCH, min(D_WINDOW_MAX, PAST_LEN), D_HEADS, HEAD_DIM)
 followed by the weights.
Output tuple: (y_prompt (BATCH, SEQ, D_MODEL), y_sample (DEC_BATCH, DEC_SEQ, D_MODEL),
 new_a_k_prompt, new_a_v_prompt (N_EVEN, BATCH, min(A_WINDOW, SEQ), A_KV_HEADS, HEAD_DIM),
 new_b_conv_prompt (N_EVEN, BATCH, CONV_WIDTH-1, B_WIDTH), new_c_pool_prompt (N_ODD, BATCH, POOL_MAX-1, C_WIDTH),
 new_d_k_prompt, new_d_v_prompt (N_ODD, BATCH, min(D_WINDOW_MAX, SEQ), D_HEADS, HEAD_DIM),
 new_a_k_sample, new_a_v_sample, new_b_conv_sample, new_c_pool_sample, new_d_k_sample, new_d_v_sample
 with leading dims DEC_BATCH in the layouts of the corresponding inputs).
"""

D_MODEL = 1024
BATCH = 1
SEQ = 1024
DEPTH = 2
DEC_BATCH = 8
DEC_SEQ = 8
PAST_LEN = 4096
PAGE_SIZE = 128

HEAD_DIM = 64
A_HEADS = 8
A_KV_HEADS = 2
A_GROUP = A_HEADS // A_KV_HEADS
A_WINDOW = 128
A_Q = A_HEADS * HEAD_DIM
A_KV = A_KV_HEADS * HEAD_DIM
B_WIDTH = D_MODEL // 2
CONV_WIDTH = 3
C_WIDTH = D_MODEL // 2
POOL_WINDOWS = (2, 4, 8, 16)
C_GROUPS = len(POOL_WINDOWS)
C_GROUP_WIDTH = C_WIDTH // C_GROUPS
POOL_MAX = max(POOL_WINDOWS)
D_HEADS = 8
D_QKV = D_HEADS * HEAD_DIM
D_BRANCHES = ((128, 1), (512, 4), (2048, 16))
D_WINDOW_MAX = max(w for w, _ in D_BRANCHES)
EVEN_IN = A_Q + 2 * A_KV + 3 * B_WIDTH
EVEN_MIX = A_Q + B_WIDTH
ODD_IN = C_WIDTH + 3 * D_QKV
ODD_MIX = C_WIDTH + D_QKV
D_MLP = 4 * D_MODEL
N_EVEN = (DEPTH + 1) // 2
N_ODD = DEPTH // 2
DEEPNORM_ALPHA = (2 * DEPTH) ** 0.25
DEEPNORM_BETA = (8 * DEPTH) ** -0.25
LN_EPS = 1e-5

kernel_name = "hybrid_swa_conv_pool_dilated_step"

def alibi_slopes(n_heads):
    return jnp.asarray(2.0 ** (-8.0 * np.arange(1, n_heads + 1) / n_heads), dtype=jnp.float32)

def layer_norm(x, g, b):
    xf = x.astype(jnp.float32)
    mu = jnp.mean(xf, axis=-1, keepdims=True)
    var = jnp.mean(jnp.square(xf - mu), axis=-1, keepdims=True)
    return ((xf - mu) * lax.rsqrt(var + LN_EPS) * g.astype(jnp.float32) + b.astype(jnp.float32)).astype(x.dtype)

def squared_relu_mlp(x, w1, w2):
    return jnp.square(jax.nn.relu(x @ w1)) @ w2

def combine_branches(parts, sink=None):
    o = jnp.stack([p[0] for p in parts])
    m = jnp.stack([p[1] for p in parts])
    s = jnp.stack([p[2] for p in parts])
    m_ref = jnp.max(m, axis=0)
    if sink is not None:
        m_ref = jnp.maximum(m_ref, sink)
    w = s * jnp.exp(m - m_ref)
    den = jnp.sum(w, axis=0)
    if sink is not None:
        den = den + jnp.exp(sink - m_ref)
    return jnp.sum(w[..., None] * o, axis=0) / den[..., None]

def banded_window_attn(q, k, v, dilation, n_w, slopes):
    B, S = q.shape[0], q.shape[1]
    n = S // dilation
    blk = n_w
    nb = -(-n // blk)
    pad = nb * blk - n

    def strided(x):
        rest = x.shape[2:]
        x = jnp.moveaxis(x.reshape((B, n, dilation) + rest), 2, 1)
        return x.reshape((B * dilation, n) + rest)

    def blocks(x):
        x = jnp.pad(x, [(0, 0), (0, pad)] + [(0, 0)] * (x.ndim - 2))
        return x.reshape((x.shape[0], nb, blk) + x.shape[2:])

    def with_prev(xb):
        prev = jnp.pad(xb[:, :-1], [(0, 0), (1, 0)] + [(0, 0)] * (xb.ndim - 2))
        return jnp.concatenate([prev, xb], axis=2)

    def unstrided(x):
        rest = x.shape[3:]
        x = x.reshape((B * dilation, nb * blk) + rest)[:, :n]
        x = jnp.moveaxis(x.reshape((B, dilation, n) + rest), 1, 2)
        return x.reshape((B, S) + rest)

    qb = blocks(strided(q))
    kk = with_prev(blocks(strided(k)))
    vv = with_prev(blocks(strided(v)))
    scores = jnp.einsum('bnqhgd,bnkhd->bnhgqk', qb, kk, preferred_element_type=jnp.float32)
    qi = jnp.arange(blk)[:, None]
    kj = jnp.arange(2 * blk)[None, :]
    dist = qi + blk - kj
    key_idx = jnp.arange(nb)[:, None, None] * blk - blk + kj[None]
    valid = (dist >= 0)[None] & (dist <= n_w)[None] & (key_idx >= 0)
    bias = -slopes[:, :, None, None] * (dist * dilation).astype(jnp.float32)[None, None]
    scores = jnp.where(valid[None, :, None, None], scores + bias[None, None], -jnp.inf)
    m = jnp.max(scores, axis=-1)
    p = jnp.exp(scores - m[..., None])
    s = jnp.sum(p, axis=-1)
    o = jnp.einsum('bnhgqk,bnkhd->bnqhgd', p, vv.astype(jnp.float32))
    m = jnp.moveaxis(m, -1, 2)
    s = jnp.moveaxis(s, -1, 2)
    o = o / s[..., None]
    return unstrided(o), unstrided(m), unstrided(s)

def gathered_window_attn(q, k_all, v_all, n_hist, dilation, n_w, slopes):
    T = q.shape[1]
    j = jnp.arange(n_w + 1)
    idx = n_hist + jnp.arange(T)[:, None] - j[None, :] * dilation
    valid = idx >= 0
    idx = jnp.maximum(idx, 0)
    kg = k_all[:, idx]
    vg = v_all[:, idx]
    scores = jnp.einsum('bthgd,btjhd->bthgj', q, kg, preferred_element_type=jnp.float32)
    bias = -slopes[:, :, None] * (j * dilation).astype(jnp.float32)[None, None]
    scores = jnp.where(valid[None, :, None, None, :], scores + bias, -jnp.inf)
    m = jnp.max(scores, axis=-1)
    p = jnp.exp(scores - m[..., None])
    s = jnp.sum(p, axis=-1)
    o = jnp.einsum('bthgj,btjhd->bthgd', p, vg.astype(jnp.float32)) / s[..., None]
    return o, m, s

def multi_pool_minus_identity(u_all, n_new, pos):
    H = u_all.shape[1] - n_new
    uf = u_all.astype(jnp.float32)
    cs = jnp.pad(jnp.cumsum(uf, axis=1), [(0, 0), (1, 0), (0, 0)])
    end = cs[:, H + 1:H + 1 + n_new]
    outs = []
    for g, w in enumerate(POOL_WINDOWS):
        lo, hi = g * C_GROUP_WIDTH, (g + 1) * C_GROUP_WIDTH
        start = cs[:, H + 1 - w:H + 1 - w + n_new, lo:hi]
        cnt = jnp.minimum(pos + 1, w).astype(jnp.float32)[:, None]
        outs.append((end[..., lo:hi] - start) / cnt - uf[:, H:, lo:hi])
    return jnp.concatenate(outs, axis=-1)

def even_mixer(x, hist, w_in, b_in, sinks, conv_w, w_out, b_out):
    Bn, T, _ = x.shape
    proj = x @ w_in + b_in
    o1 = A_Q
    o2 = o1 + A_KV
    o3 = o2 + A_KV
    o4 = o3 + B_WIDTH
    o5 = o4 + B_WIDTH
    q, k, v, h, gb, gc = jnp.split(proj, [o1, o2, o3, o4, o5], axis=-1)
    q = q.reshape(Bn, T, A_KV_HEADS, A_GROUP, HEAD_DIM) * HEAD_DIM ** -0.5
    k = k.reshape(Bn, T, A_KV_HEADS, HEAD_DIM)
    v = v.reshape(Bn, T, A_KV_HEADS, HEAD_DIM)
    c = gc * h
    slopes = alibi_slopes(A_HEADS).reshape(A_KV_HEADS, A_GROUP)
    if hist is None:
        part = banded_window_attn(q, k, v, 1, A_WINDOW, slopes)
        c_hist = jnp.zeros((Bn, CONV_WIDTH - 1, B_WIDTH), c.dtype)
        n_keep = min(A_WINDOW, T)
        new_k, new_v = k[:, -n_keep:], v[:, -n_keep:]
    else:
        k_cache, v_cache, c_hist = hist
        n_hist = k_cache.shape[1]
        k_all = jnp.concatenate([k_cache, k], axis=1)
        v_all = jnp.concatenate([v_cache, v], axis=1)
        part = gathered_window_attn(q, k_all, v_all, n_hist, 1, A_WINDOW, slopes)
        new_k, new_v = k_all[:, -n_hist:], v_all[:, -n_hist:]
    sink = sinks.astype(jnp.float32).reshape(A_KV_HEADS, A_GROUP)
    y_a = combine_branches([part], sink=sink).reshape(Bn, T, A_Q).astype(x.dtype)
    c_all = jnp.concatenate([c_hist, c], axis=1)
    conv = sum(c_all[:, i:i + T] * conv_w[i] for i in range(CONV_WIDTH))
    y_b = gb * conv
    mix = jnp.concatenate([y_a, y_b], axis=-1) @ w_out + b_out
    return mix, (new_k, new_v, c_all[:, -(CONV_WIDTH - 1):])

def odd_mixer(x, pos, hist, w_in, b_in, w_group, scale, w_out, b_out):
    Bn, T, _ = x.shape
    proj = x @ w_in + b_in
    u, q, k, v = jnp.split(proj, [C_WIDTH, C_WIDTH + D_QKV, C_WIDTH + 2 * D_QKV], axis=-1)
    q = q.reshape(Bn, T, D_HEADS, 1, HEAD_DIM) * HEAD_DIM ** -0.5
    k = k.reshape(Bn, T, D_HEADS, HEAD_DIM)
    v = v.reshape(Bn, T, D_HEADS, HEAD_DIM)
    slopes = alibi_slopes(D_HEADS).reshape(D_HEADS, 1)
    if hist is None:
        parts = [banded_window_attn(q, k, v, d, w // d, slopes) for w, d in D_BRANCHES]
        u_hist = jnp.zeros((Bn, POOL_MAX - 1, C_WIDTH), u.dtype)
        n_keep = min(D_WINDOW_MAX, T)
        new_k, new_v = k[:, -n_keep:], v[:, -n_keep:]
    else:
        u_hist, k_cache, v_cache = hist
        n_hist = k_cache.shape[1]
        k_all = jnp.concatenate([k_cache, k], axis=1)
        v_all = jnp.concatenate([v_cache, v], axis=1)
        parts = [gathered_window_attn(q, k_all, v_all, n_hist, d, w // d, slopes) for w, d in D_BRANCHES]
        new_k, new_v = k_all[:, -n_hist:], v_all[:, -n_hist:]
    y_d = combine_branches(parts).reshape(Bn, T, D_QKV).astype(x.dtype)
    u_all = jnp.concatenate([u_hist, u], axis=1)
    pooled = multi_pool_minus_identity(u_all, T, pos).astype(x.dtype)
    y_c = jnp.einsum('btgc,gcd->btgd', pooled.reshape(Bn, T, C_GROUPS, C_GROUP_WIDTH), w_group)
    y_c = y_c.reshape(Bn, T, C_WIDTH) * scale
    mix = jnp.concatenate([y_c, y_d], axis=-1) @ w_out + b_out
    return mix, (u_all[:, -(POOL_MAX - 1):], new_k, new_v)

def trunk(x, pos, caches, even_w_in, even_b_in, a_sinks, b_conv_w, even_w_out, even_b_out,
          odd_w_in, odd_b_in, c_w_group, c_scale, odd_w_out, odd_b_out,
          mlp_w1, mlp_w2, ln1_g, ln1_b, ln2_g, ln2_b):
    even_states, odd_states = [], []
    for layer in range(DEPTH):
        i = layer // 2
        if layer % 2 == 0:
            hist = None if caches is None else (caches[0][i], caches[1][i], caches[2][i])
            mix, st = even_mixer(x, hist, even_w_in[i], even_b_in[i], a_sinks[i], b_conv_w[i],
                                 even_w_out[i], even_b_out[i])
            even_states.append(st)
        else:
            hist = None if caches is None else (caches[3][i], caches[4][i], caches[5][i])
            mix, st = odd_mixer(x, pos, hist, odd_w_in[i], odd_b_in[i], c_w_group[i], c_scale[i],
                                odd_w_out[i], odd_b_out[i])
            odd_states.append(st)
        x = layer_norm(DEEPNORM_ALPHA * x + mix, ln1_g[layer], ln1_b[layer])
        x = layer_norm(DEEPNORM_ALPHA * x + squared_relu_mlp(x, mlp_w1[layer], mlp_w2[layer]),
                       ln2_g[layer], ln2_b[layer])
    a_k = jnp.stack([s[0] for s in even_states])
    a_v = jnp.stack([s[1] for s in even_states])
    b_conv = jnp.stack([s[2] for s in even_states])
    c_pool = jnp.stack([s[0] for s in odd_states])
    d_k = jnp.stack([s[1] for s in odd_states])
    d_v = jnp.stack([s[2] for s in odd_states])
    return x, a_k, a_v, b_conv, c_pool, d_k, d_v

def setup_inputs(seed: int = 0) -> dict:
    key = jax.random.key(seed)
    ks = jax.random.split(key, 26)

    def nrm(k, shape, scale):
        return jax.random.normal(k, shape, jnp.float32) * scale

    n_a = min(A_WINDOW, PAST_LEN)
    n_d = min(D_WINDOW_MAX, PAST_LEN)
    return {
        "x_prompt": nrm(ks[0], (BATCH, SEQ, D_MODEL), 1.0),
        "x_sample": nrm(ks[1], (DEC_BATCH, DEC_SEQ, D_MODEL), 1.0),
        "cache_a_k": nrm(ks[2], (N_EVEN, DEC_BATCH, n_a, A_KV_HEADS, HEAD_DIM), 1.0),
        "cache_a_v": nrm(ks[3], (N_EVEN, DEC_BATCH, n_a, A_KV_HEADS, HEAD_DIM), 1.0),
        "state_b_conv": nrm(ks[4], (N_EVEN, DEC_BATCH, CONV_WIDTH - 1, B_WIDTH), 1.0),
        "state_c_pool": nrm(ks[5], (N_ODD, DEC_BATCH, POOL_MAX - 1, C_WIDTH), 1.0),
        "cache_d_k": nrm(ks[6], (N_ODD, DEC_BATCH, n_d, D_HEADS, HEAD_DIM), 1.0),
        "cache_d_v": nrm(ks[7], (N_ODD, DEC_BATCH, n_d, D_HEADS, HEAD_DIM), 1.0),
        "even_w_in": nrm(ks[8], (N_EVEN, D_MODEL, EVEN_IN), D_MODEL ** -0.5),
        "even_b_in": nrm(ks[9], (N_EVEN, EVEN_IN), 0.02),
        "a_sinks": nrm(ks[10], (N_EVEN, A_HEADS), 1.0),
        "b_conv_w": nrm(ks[11], (N_EVEN, CONV_WIDTH, B_WIDTH), CONV_WIDTH ** -0.5),
        "even_w_out": nrm(ks[12], (N_EVEN, EVEN_MIX, D_MODEL), EVEN_MIX ** -0.5 * DEEPNORM_BETA),
        "even_b_out": nrm(ks[13], (N_EVEN, D_MODEL), 0.02),
        "odd_w_in": nrm(ks[14], (N_ODD, D_MODEL, ODD_IN), D_MODEL ** -0.5),
        "odd_b_in": nrm(ks[15], (N_ODD, ODD_IN), 0.02),
        "c_w_group": nrm(ks[16], (N_ODD, C_GROUPS, C_GROUP_WIDTH, C_GROUP_WIDTH), C_GROUP_WIDTH ** -0.5),
        "c_scale": 1.0 + nrm(ks[17], (N_ODD, C_WIDTH), 0.1),
        "odd_w_out": nrm(ks[18], (N_ODD, ODD_MIX, D_MODEL), ODD_MIX ** -0.5 * DEEPNORM_BETA),
        "odd_b_out": nrm(ks[19], (N_ODD, D_MODEL), 0.02),
        "mlp_w1": nrm(ks[20], (DEPTH, D_MODEL, D_MLP), D_MODEL ** -0.5),
        "mlp_w2": nrm(ks[21], (DEPTH, D_MLP, D_MODEL), D_MLP ** -0.5 * DEEPNORM_BETA),
        "ln1_g": 1.0 + nrm(ks[22], (DEPTH, D_MODEL), 0.05),
        "ln1_b": nrm(ks[23], (DEPTH, D_MODEL), 0.02),
        "ln2_g": 1.0 + nrm(ks[24], (DEPTH, D_MODEL), 0.05),
        "ln2_b": nrm(ks[25], (DEPTH, D_MODEL), 0.02),
    }

def reference(x_prompt, x_sample, cache_a_k, cache_a_v, state_b_conv, state_c_pool, cache_d_k, cache_d_v,
              even_w_in, even_b_in, a_sinks, b_conv_w, even_w_out, even_b_out,
              odd_w_in, odd_b_in, c_w_group, c_scale, odd_w_out, odd_b_out,
              mlp_w1, mlp_w2, ln1_g, ln1_b, ln2_g, ln2_b):
    weights = (even_w_in, even_b_in, a_sinks, b_conv_w, even_w_out, even_b_out,
               odd_w_in, odd_b_in, c_w_group, c_scale, odd_w_out, odd_b_out,
               mlp_w1, mlp_w2, ln1_g, ln1_b, ln2_g, ln2_b)
    pos_prompt = jnp.arange(x_prompt.shape[1])
    pos_sample = PAST_LEN + jnp.arange(x_sample.shape[1])
    y_prompt, ak_p, av_p, bc_p, cp_p, dk_p, dv_p = trunk(x_prompt, pos_prompt, None, *weights)
    sample_caches = (cache_a_k, cache_a_v, state_b_conv, state_c_pool, cache_d_k, cache_d_v)
    y_sample, ak_s, av_s, bc_s, cp_s, dk_s, dv_s = trunk(x_sample, pos_sample, sample_caches, *weights)
    return (y_prompt, y_sample, ak_p, av_p, bc_p, cp_p, dk_p, dv_p, ak_s, av_s, bc_s, cp_s, dk_s, dv_s)


_drawn_inputs = setup_inputs


def setup_inputs(seed=0):
    import zlib

    import numpy as np

    out = dict(_drawn_inputs(seed))
    spreads = {}
    factors = {'a_sinks': 3.552,
     'even_b_out': 3.854,
     'odd_b_in': 2.7,
     'c_scale': 2.716,
     'odd_b_out': 4.033}
    for name, (base, spread) in spreads.items():
        noise = np.random.default_rng([zlib.crc32(name.encode()), seed]).standard_normal(out[name].shape)
        drawn = base * np.exp(spread * noise) if base else spread * noise
        out[name] = __import__('jax').numpy.asarray(drawn.astype(out[name].dtype))
    for name, factor in factors.items():
        out[name] = (out[name] * factor).astype(out[name].dtype)
    return out
```

```python
import numpy as np
import concourse.bass as bass
from concourse import mybir
from contextlib import ExitStack

P = 128
D_MODEL, SEQ, DEC_BATCH, DEC_SEQ = 1024, 1024, 8, 8
NS = DEC_BATCH * DEC_SEQ
NT = SEQ + NS
KC = D_MODEL // P
HD = 64
A_HEADS, A_WINDOW = 8, 128
B_WIDTH, CONV_W = 512, 3
D_HEADS = 8
D_BRANCHES = ((128, 1), (512, 4), (2048, 16))
D_WINDOW = 2048
POOL_WINDOWS = (2, 4, 8, 16)
POOL_HIST = 15
ALPHA = float(4 ** 0.25)
EPS = 1e-5
QSCALE = HD ** -0.5
NEG = -1.0e30
N_HB = 8

GROUP = ((0, 384), (384, 384), (768, 320))
TILE_COLS = P
N_TILES = 9

EVEN_IN, EVEN_OUT, MLP_TILES, ODD_IN, ODD_OUT = 18, 8, 64, 16, 8
T_EIN = 0
T_EOUT = T_EIN + EVEN_IN
T_MLP = (T_EOUT + EVEN_OUT, T_EOUT + EVEN_OUT + MLP_TILES + ODD_IN + ODD_OUT)
T_OIN = T_MLP[0] + MLP_TILES
T_OOUT = T_OIN + ODD_IN
W_TILES = T_MLP[1] + MLP_TILES
NSLOT = 4
NRAW = 2

C_EBIN = 0
C_CONV = C_EBIN + EVEN_IN
C_EBOUT = C_CONV + CONV_W * 4
C_OBIN = C_EBOUT + KC
C_CSCALE = C_OBIN + ODD_IN
C_OBOUT = C_CSCALE + 4
C_LNG = C_OBOUT + KC
C_LNB = C_LNG + 4 * KC
N_COLS = C_LNB + 4 * KC

U_EIN = 0
U_EOUT = U_EIN + 3 * EVEN_IN
U_MLP = (U_EOUT + 3 * EVEN_OUT, U_EOUT + 3 * EVEN_OUT + N_HB * 24 + 3 * ODD_IN + 12 + 3 * ODD_OUT)
U_OIN = U_MLP[0] + N_HB * 24
U_OOUT = U_OIN + 3 * ODD_IN + 12
H_UNITS = 12 * N_HB

XS_IN, XS_MIX0, XS_LN0, XS_LN1, XS_MIX1, XS_LN2 = 0, 3, 6, 30, 54, 57
XS_LN = (XS_LN0, XS_LN1, XS_LN2)

NB_D = 10
KEYS_D = NB_D * P + NS
N_JOBS_A = 17


def unit_done_ein(t):
    s, j = divmod(t, 4)
    return U_EIN + 12 * s + (8 + j + 1 if s < 4 else 4 + j + 1)


def build(nc, io):
    F32, F32R = mybir.dt.float32, mybir.dt.float32r
    ALU, ACT, AX = mybir.AluOpType, mybir.ActivationFunctionType, mybir.AxisListType
    ctx = ExitStack()
    with ctx:
        place = [nc.sbuf_base + (-nc.sbuf_base) % 64]

        def at(name, shape, dtype, offset):
            return nc.alloc_sbuf_tensor_at(name, shape, dtype, offset=offset)

        def room(nbytes):
            o = place[0]
            place[0] += -(-nbytes // 64) * 64
            return o

        def small(name, shape):
            n = 4
            for s in shape[1:]:
                n *= s
            return at(name, shape, F32, room(n))

        R = KC * NT * 4
        o_xr, o_hr, o_xs = room(R), room(R), room(2 * R)
        o_ws, o_wr, o_scr = room(NSLOT * 8192), room(NRAW * 4096), room(18432)

        X = at("X", [P, KC, NT], F32, o_xr)
        XS = at("XS", [P, 2, KC, NT], F32R, o_xs)
        HID = at("HID", [P, 2, 4, NT], F32R, o_hr)
        Y = at("Y", [P, KC, NT], F32, o_hr)
        WS = at("WS", [P, NSLOT, 2, 1024], F32R, o_ws)
        WR = at("WR", [P, NRAW, 1024], F32, o_wr)
        ZN = at("ZN", [P, 3, 1024], F32, o_scr)
        RT = at("RT", [P, 2, 384], F32, o_scr + 12288)
        ST = at("ST", [P, 2, 384], F32, o_scr + 15360)
        q = o_xr
        KTA = at("KTA", [P, NT], F32, q)
        VA = at("VA", [P, N_TILES, P], F32, q + 4352)
        CB = at("CB", [P, 2 + SEQ], F32, q + 8960)
        CV = at("CV", [P, NT], F32, q + 8960 + 4160)
        HT = at("HT", [P, NT], F32, q + 8960 + 4160 + 4352)
        KCT = at("KCT", [P, DEC_BATCH, P], F32, q + 21824)
        VCA = at("VCA", [P, DEC_BATCH, P], F32, q + 25920)
        KCA = at("KCA", [P, DEC_BATCH, P], F32, o_hr + R // 2)
        BAS = at("BAS", [P, 4, 192], F32, q + 30016)
        QS = at("QS", [P, DEC_BATCH, 4, DEC_SEQ], F32, q + 33088)
        SMA = at("SMA", [P, 4, 256], F32, o_scr)
        PTA = at("PTA", [P, 8, P], F32, o_scr + 4096)
        OTA = at("OTA", [P, 4, P], F32, o_scr + 8192)
        BA = at("BA", [P, 2, 4, 256], F32, o_scr + 10240)
        VT0 = at("VT0", [P, 2, 384], F32, o_scr)
        KTD = at("KTD", [P, 4, NT], F32, o_xr)
        VD = at("VD", [P, 8, 512], F32, o_xr + R // 2)
        PA = at("PA", [P, 16 + SEQ], F32, o_scr)
        PB = at("PB", [P, 16 + SEQ], F32, o_scr + 4160)
        PO = at("PO", [P, NT], F32, o_scr + 8320)
        SA = at("SA", [P, DEC_BATCH, 23], F32, o_scr + 12672)
        SB = at("SB", [P, DEC_BATCH, 23], F32, o_scr + 13408)
        VT1 = at("VT1", [P, 2, 384], F32, o_scr + 14144)
        TH = at("TH", [P, 2, SEQ], F32, o_xs)
        SMD = at("SMD", [P, 2, SEQ], F32, o_xs + 8192)
        PTD = at("PTD", [P, 2, 8, P], F32, o_xs + 16384)
        OTD = at("OTD", [P, 8, P], F32, o_xs + 24576)
        KCD = at("KCD", [P, NB_D, 512], F32, o_xs + 28672)
        VCD = at("VCD", [P, NB_D, 512], F32, o_xs + 49152)
        KTC = at("KTC", [P, 2, NB_D * P], F32, o_xs)
        SMS = at("SMS", [P, KEYS_D], F32, o_xs + 10240)
        PTS = at("PTS", [P, NB_D + 1, P], F32, o_xs + 15616)
        BS = at("BS", [P, KEYS_D], F32, o_xs + 21248)
        QBD = at("QBD", [P, 2, 4, 32], F32, o_xs + 26624)
        BNEW = at("BNEW", [P, DEC_BATCH, NS], F32, o_scr)
        IDN = small("IDN", [P, P])
        COLS = small("COLS", [P, N_COLS])
        SINK = small("SINK", [P, 12])
        RC = small("RC", [P, 4, 16])
        CS = small("CS", [P, 4, DEC_BATCH, 2 + DEC_SEQ])
        BCO = small("BCO", [P, 4, 2])
        KN = small("KN", [NS, 512])
        VN = small("VN", [NS, 512])
        US = small("US", [P, 4, DEC_BATCH, POOL_HIST + DEC_SEQ])
        UO = small("UO", [P, 4, POOL_HIST])
        BNS = small("BNS", [P, 12])
        MV = small("MV", [P, 2])
        VE = small("VE", [P, 1])
        SD = small("SD", [P, 1])
        RS = small("RS", [P, 1])
        NW = small("NW", [P, 1])
        MX = small("MX", [P, 2, 4])
        NM = small("NM", [P, 2, 4])
        DS = small("DS", [P, 4])
        ES = small("ES", [P, 4])
        SUM = small("SUM", [P, 2, 4])
        RD = small("RD", [P, 2, 4])
        GW = small("GW", [P, 4, P])
        assert place[0] <= nc.sbuf_top, (place[0], nc.sbuf_top)

        PS = ctx.enter_context(nc.psum_tensor("PS", [P, 8, 512], F32))
        FT = PS[:, 0:2, :].rearrange("p a b -> p (a b)")

        def bank(b, n=512):
            return PS[:, b, 0:n]

        def sem(name):
            return ctx.enter_context(nc.semaphore(name))

        x_in = [sem(f"x_in{g}") for g in range(3)]
        xr_in = [[sem(f"xr{l}_in{g}") for g in range(3)] for l in range(2)]
        spilled = sem("spilled")
        ident_in, cols_in, kca_in, biasa_in = sem("ident_in"), sem("cols_in"), sem("kca_in"), sem("biasa_in")
        states_in, qs_ready, bas_in, vca_in = sem("states_in"), sem("qs_ready"), sem("bas_in"), sem("vca_in")
        w_in = [sem(f"w_in{r}") for r in range(NRAW)]
        w_hi, w_split = sem("w_hi"), sem("w_split")
        p_mm, p_evac = sem("p_mm"), sem("p_evac")
        h_mm, h_evac, h_sq, hid_hi, hid_ready = sem("h_mm"), sem("h_evac"), sem("h_sq"), sem("hid_hi"), sem("hid_ready")
        x_hi, x_split, x_scaled = sem("x_hi"), sem("x_split"), sem("x_scaled")
        ft_mm, ve_ready, std_ready, zn_ready = sem("ft_mm"), sem("ve_ready"), sem("std_ready"), sem("zn_ready")
        bt_mm, b_evac, b_hi = sem("bt_mm"), sem("b_evac"), sem("b_hi")
        dve_link, vt_mm, vt_evac = sem("dve_link"), sem("vt_mm"), sem("vt_evac")
        kn_mm, kn_evac = sem("kn_mm"), sem("kn_evac")
        kct_mm, kct_evac = sem("kct_mm"), sem("kct_evac")
        sa_mm, sa_max, sa_exp, sa_prob, pta_mm, pta_evac = (sem("sa_mm"), sem("sa_max"), sem("sa_exp"),
                                                            sem("sa_prob"), sem("pta_mm"), sem("pta_evac"))
        oa_mm, oa_evac, ota_mm, ota_evac = sem("oa_mm"), sem("oa_evac"), sem("ota_mm"), sem("ota_evac")
        th_in = [sem("th_in0"), sem("th_in1")]
        sd_mm, sd_max, sd_exp, ptd_mm, ptd_evac = sem("sd_mm"), sem("sd_max"), sem("sd_exp"), sem("ptd_mm"), sem("ptd_evac")
        od_mm, od_evac = sem("od_mm"), sem("od_evac")
        ks_in, vs_in, bs_in = sem("ks_in"), sem("vs_in"), sem("bs_in")
        ktc_mm, ktc_evac, qbd_ready, ss_mm, ss_max, ss_exp, ss_prob = (
            sem("ktc_mm"), sem("ktc_evac"), sem("qbd_ready"), sem("ss_mm"), sem("ss_max"), sem("ss_exp"), sem("ss_prob"))
        pts_mm, pts_evac, os_mm, os_evac = sem("pts_mm"), sem("pts_evac"), sem("os_mm"), sem("os_evac")
        bco_ready, uo_ready, qbd_zero, po_ready = sem("bco_ready"), sem("uo_ready"), sem("qbd_zero"), sem("po_ready")
        copied, stored_a, stored_d, stored_y = sem("copied"), sem("stored_a"), sem("stored_d"), sem("stored_y")

        def col(i, n=P):
            return COLS[0:n, i:i + 1]

        def tile_rows(t):
            return NS if t == N_TILES - 1 else P

        def job_a(n):
            qb, half = divmod(n, 2)
            if n == N_JOBS_A - 1:
                return 192, 2, 0
            return (P, 1, 0) if qb == 0 else (2 * P, 2, (qb - 1) * P)

        def pieces_d(m):
            nk = m % 8 + 1
            return [(k, min(4, nk - k)) for k in range(0, nk, 4)]

        piece_base = [0]
        for m in range(64):
            extra = 2 if m % 16 == 15 else 0
            piece_base.append(piece_base[-1] + len(pieces_d(m)) + extra)

        block = ctx.enter_context(nc.Block())

        @block.sync
        def _(sp):
            def weight(t, first=0):
                if t >= NRAW:
                    sp.wait_ge(w_split, t - NRAW + 1)
                sp.dma_start(WR[:, t % NRAW, :], io["w"][t, :, :]).then_inc(w_in[t % NRAW], 16)

            def weight_loop(i, t0, j):
                t = 8 * i + (t0 + j)
                sp.wait_ge(w_split, t - NRAW + 1)
                sp.dma_start(WR[:, (t0 + j) % NRAW, :],
                             io["w"][bass.ds(t, 1), :, :].rearrange("a p n -> (a p) n")).then_inc(w_in[(t0 + j) % NRAW], 16)

            for t in range(2):
                weight(t)
            for g, (c0, gw) in enumerate(GROUP):
                sp.dma_start(X[:, :, c0:c0 + gw], io["x"][:, :, c0:c0 + gw]).then_inc(x_in[g], 16)
            for t in range(2, T_EOUT + 6):
                weight(t)
            sp.wait_ge(ota_evac, 10)
            sp.wait_ge(p_evac, U_EOUT)
            sp.wait_ge(kn_evac, 1)
            sp.wait_ge(bco_ready, 4)
            sp.dma_start(io["a_k"][:, :], KTA[:, SEQ - A_WINDOW:SEQ]).then_inc(stored_a, 16)
            sp.dma_start(io["a_v"][:, :], VA[:, 7, :]).then_inc(stored_a, 16)
            for b in range(DEC_BATCH):
                rows = slice(b * DEC_SEQ, (b + 1) * DEC_SEQ)
                sp.dma_start(io["a_ks"][b, A_WINDOW - DEC_SEQ:, :], KN[rows, 0:P]).then_inc(stored_a, 16)
                sp.dma_start(io["a_vs"][b, A_WINDOW - DEC_SEQ:, :], VA[rows, 8, :]).then_inc(stored_a, 16)
            sp.dma_start(io["b_c"][:, :, :], BCO[:, :, :]).then_inc(stored_a, 16)
            for j in range(4):
                sp.dma_start(io["b_cs"][:, j, :, :], CS[:, j, :, DEC_SEQ:]).then_inc(stored_a, 16)
            sp.wait_ge(stored_a, 16 * 23)
            for g, (c0, gw) in enumerate(GROUP):
                sp.dma_start(X[:, :, c0:c0 + gw], io["x"][:, :, c0:c0 + gw]).then_inc(xr_in[0][g], 16)
            for t in range(T_EOUT + 6, T_MLP[0] + 4):
                weight(t)
            with sp.Fori(0, N_HB - 1) as i:
                for j in range(8):
                    weight_loop(i, T_MLP[0] + 4, j)
            for t in range(T_OIN - 4, T_OIN + 6):
                weight(t)
            for g, (c0, gw) in enumerate(GROUP):
                sp.wait_ge(x_scaled, 24 + 8 * (g + 1))
                sp.dma_start(io["spill"][:, :, c0:c0 + gw], X[:, :, c0:c0 + gw]).then_inc(spilled, 16)
            for t in range(T_OIN + 6, T_OIN + ODD_IN):
                weight(t)
            sp.wait_ge(p_mm, U_OIN + 36 + 18)
            for h in range(2):
                sp.dma_start(TH[:, h, :], io["th"][h, :, :]).then_inc(th_in[h], 16)

            def load_cache(dst, name, b, done):
                far = io[name][b, :, :].rearrange("(a s) f -> a s f", s=16)
                sp.dma_start(dst[:, 0:8, :], far[:, 0:8, :]).then_inc(done, 16)
                for r in range(4):
                    sp.dma_start(dst[32 * r:32 * r + 32, 8:10, :], far[96:128, 8 + 2 * r:10 + 2 * r, :]).then_inc(done, 16)

            load_cache(KCD, "cache_d_k", 0, ks_in)
            load_cache(VCD, "cache_d_v", 0, vs_in)
            for t in range(T_OOUT, T_OOUT + 2):
                weight(t)
            for h in range(2, D_HEADS):
                sp.wait_ge(sd_max, 8 * (h - 1))
                sp.dma_start(TH[:, h % 2, :], io["th"][h, :, :]).then_inc(th_in[h % 2], 16)
            for t in range(T_OOUT + 2, T_OOUT + 6):
                weight(t)
            sp.wait_ge(ptd_evac, piece_base[64])
            sp.wait_ge(od_evac, 64)
            sp.dma_start(BS[:, 0:NB_D * P], io["bs"][:, :]).then_inc(bs_in, 16)
            sp.dma_start(BNEW[:, :, :], io["bnew"][:, :, :]).then_inc(bs_in, 16)
            sp.wait_ge(kn_evac, 2)
            sp.wait_ge(uo_ready, 4)
            for c in range(4):
                sp.dma_start(io["d_k"][:, c, :], KTD[:, c, 0:SEQ]).then_inc(stored_d, 16)
            sp.dma_start(io["d_v"].rearrange("(t p) f -> p t f", p=P), VD[:, :, :]).then_inc(stored_d, 16)
            for b in range(DEC_BATCH):
                rows = slice(b * DEC_SEQ, (b + 1) * DEC_SEQ)
                sp.dma_start(io["d_ks"][b, D_WINDOW - DEC_SEQ:, :], KN[rows, :]).then_inc(stored_d, 16)
                sp.dma_start(io["d_vs"][b, D_WINDOW - DEC_SEQ:, :], VN[rows, :]).then_inc(stored_d, 16)
            sp.dma_start(io["c_p"][:, :, :], UO[:, :, :]).then_inc(stored_d, 16)
            for c in range(4):
                sp.dma_start(io["c_ps"][:, c, :, :], US[:, c, :, DEC_SEQ:]).then_inc(stored_d, 16)
            for b in range(1, DEC_BATCH + 1):
                if b < DEC_BATCH:
                    sp.wait_ge(ktc_mm, 12 * b)
                    load_cache(KCD, "cache_d_k", b, ks_in)
                if b >= 2:
                    sp.wait_ge(os_mm, b - 1)
                    load_cache(VCD, "cache_d_v", b - 1, vs_in)
            sp.wait_ge(stored_d, 16 * 26)
            sp.wait_ge(os_evac, DEC_BATCH)
            sp.wait_ge(spilled, 48)
            for g, (c0, gw) in enumerate(GROUP):
                sp.dma_start(X[:, :, c0:c0 + gw], io["spill"][:, :, c0:c0 + gw]).then_inc(xr_in[1][g], 16)
            for t in range(T_OOUT + 6, T_MLP[1] + 4):
                weight(t)
            with sp.Fori(0, N_HB - 1) as i:
                for j in range(8):
                    weight_loop(i, T_MLP[1] + 4, j)
            for t in range(W_TILES - 4, W_TILES):
                weight(t)
            for g, (c0, gw) in enumerate(GROUP):
                sp.wait_ge(b_evac, 72 + 8 * (g + 1))
                sp.dma_start(io["y"][:, :, c0:c0 + gw], X[:, :, c0:c0 + gw]).then_inc(stored_y, 16)
            sp.wait_ge(stored_y, 48)
            sp.wait_ge(copied, 16 * 18)

        @block.gpsimd
        def _(pool):
            def split(t, slot, raw):
                pool.wait_ge(w_in[raw], 16 * (t // NRAW + 1) if isinstance(t, int) else t)
                pool.tensor_copy(WS[:, slot, 0, :], WR[:, raw, :]).then_inc(w_hi, 1)

            def rest(slot, raw, hi):
                pool.wait_ge(w_hi, hi)
                pool.tensor_tensor(WS[:, slot, 1, :], WR[:, raw, :], WS[:, slot, 0, :].bitcast(F32),
                                   ALU.subtract).then_inc(w_split, 1)

            def one(t):
                split(t, t % NSLOT, t % NRAW)
                rest(t % NSLOT, t % NRAW, t + 1)

            for t in range(NSLOT):
                one(t)
            for t in range(NSLOT, T_MLP[0]):
                was = t - NSLOT
                if was < T_EOUT:
                    pool.wait_ge(p_mm, unit_done_ein(was))
                else:
                    pool.wait_ge(p_mm, U_EOUT + 8 + (was - T_EOUT) + 1)
                one(t)

            def mlp(l):
                t0 = T_MLP[l]
                for j in range(4):
                    pool.wait_ge(p_mm, U_MLP[l] - 4 + j + 1)
                    one(t0 + j)
                with pool.Fori(0, N_HB - 1) as i:
                    for j in range(8):
                        slot, raw = (t0 + j) % NSLOT, (t0 + j) % NRAW
                        if j < 4:
                            pool.wait_ge(h_mm, 12 * i + (H_UNITS * l + 8 + j + 1))
                        else:
                            pool.wait_ge(p_mm, 24 * i + (U_MLP[l] + 16 + 2 * (j - 4) + 2))
                        pool.wait_ge(w_in[raw], 64 * i + 16 * ((t0 + 4 + j) // NRAW + 1))
                        pool.nop(nofuse=True)
                        pool.tensor_copy(WS[:, slot, 0, :], WR[:, raw, :]).then_inc(w_hi, 1)
                        rest(slot, raw, 8 * i + (t0 + 4 + j + 1))
                for j in range(4):
                    pool.wait_ge(h_mm, H_UNITS * (l + 1) - 4 + j + 1)
                    one(t0 + 60 + j)

            mlp(0)
            for t in range(T_OIN, T_MLP[1]):
                was = t - NSLOT
                if was < T_OIN:
                    pool.wait_ge(p_mm, U_OIN - 8 + 2 * (t - T_OIN) + 2)
                elif was < T_OOUT:
                    s, j = divmod(was - T_OIN, 4)
                    pool.wait_ge(p_mm, U_OIN + 12 * s + (8 if s < 3 else 14) + j + 1)
                else:
                    pool.wait_ge(p_mm, U_OOUT + 8 + (was - T_OOUT) + 1)
                one(t)
            mlp(1)

        @block.scalar
        def _(act):
            act.dma_start(IDN[:, :], io["ident"][:, :]).then_inc(ident_in, 16)
            act.dma_start(COLS[:, :], io["cols"][:, :]).then_inc(cols_in, 16)
            act.dma_start(SINK[:, :], io["sink"][:, :]).then_inc(cols_in, 16)
            act.dma_start(RC[:, :, :], io["rc"][:, :, :]).then_inc(cols_in, 16)
            act.dma_start(GW[:, :, :], io["gw"][:, :, :]).then_inc(cols_in, 16)
            act.dma_start(KCA[:, :, :], io["cache_a_k"].rearrange("b p f -> p b f")).then_inc(kca_in, 16)
            for j in range(4):
                act.dma_start(CS[:, j, :, 0:2], io["b_state"][:, j, :, :]).then_inc(states_in, 16)
                act.dma_start(US[:, j, :, 0:POOL_HIST], io["c_state"][:, j, :, :]).then_inc(states_in, 16)
            act.dma_start(BA[:, :, :, :], io["ba"][:, :, :, :]).then_inc(biasa_in, 16)
            act.dma_start(io["a_ks"][:, 0:A_WINDOW - DEC_SEQ, :], io["cache_a_k"][:, DEC_SEQ:, :]).then_inc(copied, 16)
            act.dma_start(io["a_vs"][:, 0:A_WINDOW - DEC_SEQ, :], io["cache_a_v"][:, DEC_SEQ:, :]).then_inc(copied, 16)

            def split_high(stage, src):
                for g, (c0, gw) in enumerate(GROUP):
                    if stage == 0:
                        act.wait_ge(x_in[g], 16)
                    act.activation(XS[:, 0, :, c0:c0 + gw], src[:, :, c0:c0 + gw], ACT.Copy).then_inc(x_hi, 1)

            split_high(0, X)
            act.wait_ge(x_split, 3)
            act.dma_start(VCA[:, :, :], io["cache_a_v"].rearrange("b p f -> p b f")).then_inc(vca_in, 16)
            act.dma_start(BAS[:, :, :], io["bas"][:, :, :]).then_inc(bas_in, 16)

            def ln_weave(l, phase, quarter):
                if 0 <= phase - 2 <= 2 and quarter < 2:
                    g = phase - 2
                    c0, gw = GROUP[g]
                    for k in range(4 * quarter, 4 * quarter + 4):
                        n = 24 * l + 8 * g + k
                        act.wait_ge(bt_mm, n + 1)
                        act.activation(X[:, k, c0:c0 + gw], bank(2 + n % 2, gw), ACT.Identity,
                                       scale=col(C_LNG + KC * l + k), bias=col(C_LNB + KC * l + k)).then_inc(b_evac, 1)
                        if l < 3:
                            act.wait_ge(b_evac, n + 1)
                            act.activation(XS[:, 0, k, c0:c0 + gw], X[:, k, c0:c0 + gw], ACT.Copy).then_inc(b_hi, 1)
                if 0 <= phase - 1 <= 2 and quarter > 0:
                    n = 9 * l + 3 * (phase - 1) + quarter - 1
                    rows = tile_rows(3 * (phase - 1) + quarter - 1)
                    act.wait_ge(ve_ready, n + 1)
                    act.activation(SD[0:rows, :], VE[0:rows, :], ACT.Sqrt).then_inc(std_ready, 1)

            def v_evac(n, g, dst, last):
                act.wait_ge(vt_mm, n + 1)
                b = PS[:, 4 + n % 2, 0:384].rearrange("p (t f) -> p t f", t=3)
                if g < 2:
                    act.activation(dst, b, ACT.Copy).then_inc(vt_evac, 1)
                else:
                    act.activation(dst, b[:, 0:2, :], ACT.Copy)
                    act.activation(last, b[0:NS, 2, :], ACT.Copy).then_inc(vt_evac, 1)

            act.wait_ge(x_split, 3)
            for h in range(2):
                act.wait_ge(kct_mm, h + 1)
                act.activation(KCT[:, 4 * h:4 * h + 4, :],
                               PS[:, 2 + h, :].rearrange("p (b f) -> p b f", b=4), ACT.Copy).then_inc(kct_evac, 1)
            for g in range(3):
                nt = 3 if g < 2 else 2
                v_evac(g, g, VA[:, 3 * g:3 * g + nt, :], VA[0:NS, 8, :])
            act.wait_ge(kn_mm, 1)
            act.activation(KN[:, 0:P], PS[0:NS, 4, 0:P], ACT.Copy).then_inc(kn_evac, 1)

            def a_exp(n):
                w, nk, k0 = job_a(n)
                act.wait_ge(sa_max, n + 1)
                act.activation(ES[:, :], DS[:, :], ACT.Exp)
                for c in range(4):
                    ins = act.activation(SMA[:, c, 0:w], SMA[:, c, 0:w], ACT.Exp, bias=NM[:, 0, c:c + 1],
                                         accum_out=SUM[:, 0, c:c + 1])
                ins.then_inc(sa_exp, 1)

            def a_pt(n):
                w, nk, k0 = job_a(n)
                act.wait_ge(pta_mm, n + 1)
                src = PS[:, 2:4, :].rearrange("p a (b f) -> p (a b) f", f=P)
                if n < N_JOBS_A - 1:
                    act.activation(PTA[:, 0:4 * nk, :], src[:, 0:4 * nk, :], ACT.Copy).then_inc(pta_evac, 1)
                else:
                    act.activation(PTA[:, 0:4, :], src[:, 0:4, :], ACT.Copy)
                    act.activation(PTA[0:NS, 4:8, :], src[0:NS, 4:8, :], ACT.Copy).then_inc(pta_evac, 1)

            def a_out(qb):
                act.wait_ge(ota_mm, qb + 1)
                act.activation(Y[:, 0:4, qb * P:qb * P + P], PS[:, 5, :].rearrange("p (c f) -> p c f", c=4),
                               ACT.Copy).then_inc(ota_evac, 1)

            for n in range(N_JOBS_A):
                a_exp(n)
                a_pt(n)
                if n >= 2 and n % 2 == 0:
                    a_out(n // 2 - 1)
            for quad in range(2):
                act.wait_ge(ota_mm, 9)
                for bb in range(4):
                    b = 4 * quad + bb
                    ins = act.activation(Y[:, 0:4, SEQ + 8 * b:SEQ + 8 * b + 8],
                                         PS[:, 5, P * quad + 32 * bb:P * quad + 32 * bb + 32].rearrange("p (c i) -> p c i", c=4),
                                         ACT.Copy)
                ins.then_inc(ota_evac, 1)
            act.wait_ge(ota_evac, 10)
            act.wait_ge(p_evac, U_EOUT)
            split_high(1, Y)

            def hidden_super(l, i, weave):
                for g, (c0, gw) in enumerate(GROUP):
                    for j in range(4):
                        u = 4 * g + j
                        n = 12 * i + (H_UNITS * l + u)
                        act.wait_ge(h_mm, n + 1)
                        act.activation(RT[:, u % 2, 0:gw], bank(4 + u % 2, gw), ACT.Relu).then_inc(h_evac, 1)
                        act.wait_ge(h_evac, n + 1)
                        if not (isinstance(n, int) and n < 2):
                            act.wait_ge(hid_ready, n - 1)
                        act.activation(ST[:, u % 2, 0:gw], RT[:, u % 2, 0:gw], ACT.Square).then_inc(h_sq, 1)
                        act.wait_ge(h_sq, n + 1)
                        act.activation(HID[:, 0, j, c0:c0 + gw], ST[:, u % 2, 0:gw], ACT.Copy).then_inc(hid_hi, 1)
                        if weave is not None and g < 2:
                            ln_weave(weave, 3 + g, j)

            def cache_copy(name, out, b):
                if isinstance(b, int):
                    src, dst = io[name][b], io[out][b]
                    act.dma_start(dst[0:D_WINDOW - DEC_SEQ, :], src[DEC_SEQ:, :]).then_inc(copied, 16)
                else:
                    src = io[name][bass.ds(b, 1), DEC_SEQ:, :].rearrange("a s f -> (a s) f")
                    dst = io[out][bass.ds(b, 1), 0:D_WINDOW - DEC_SEQ, :].rearrange("a s f -> (a s) f")
                    act.dma_start(dst, src).then_inc(copied, 16)

            def mlp(l, name, out):
                for g in range(3):
                    for j in range(4):
                        ln_weave(2 * l, g, j)
                hidden_super(l, 0, 2 * l)
                with act.Fori(0, N_HB - 1) as i:
                    cache_copy(name, out, i)
                    hidden_super(l, i + 1, None)
                cache_copy(name, out, N_HB - 1)
                for g in range(3):
                    for j in range(4):
                        ln_weave(2 * l + 1, g, j)

            mlp(0, "cache_d_k", "d_ks")
            for g in range(2):
                for j in range(4):
                    ln_weave(1, 3 + g, j)
            for g in range(3):
                nt = 3 if g < 2 else 2
                for j in range(4):
                    v_evac(3 + 4 * g + j, g, VD[:, 3 * g:3 * g + nt, j * P:j * P + P], VN[0:NS, j * P:j * P + P])
            act.wait_ge(kn_mm, 2)
            act.activation(KN[:, :], PS[0:NS, 3, :], ACT.Copy).then_inc(kn_evac, 1)

            def d_exp(m):
                w = P * (m % 8 + 1)
                act.wait_ge(sd_max, m + 1)
                act.activation(SMD[:, m % 2, 0:w], SMD[:, m % 2, 0:w], ACT.Exp, bias=NM[:, m % 2, 0:1],
                               accum_out=SUM[:, m % 2, 0:1]).then_inc(sd_exp, 1)

            d_exp(0)
            for m in range(64):
                if m + 1 < 64:
                    d_exp(m + 1)
                for e, (k, nk) in enumerate(pieces_d(m)):
                    n = piece_base[m] + e
                    act.wait_ge(ptd_mm, n + 1)
                    act.activation(PTD[:, m % 2, k:k + nk, :], PS[:, 4 + n % 2, 0:nk * P].rearrange("p (b f) -> p b f", f=P),
                                   ACT.Copy).then_inc(ptd_evac, 1)
                if m % 16 == 15:
                    for e in range(2):
                        n = piece_base[m + 1] - 2 + e
                        act.wait_ge(ptd_mm, n + 1)
                        act.activation(Y[:, 4 + m // 16, 512 * e:512 * e + 512], bank(4 + n % 2), ACT.Copy)\
                           .then_inc(ptd_evac, 1)
            def q_block_diag(b):
                s = b % 2
                act.activation(QBD[0:HD, s, :, 0:DEC_SEQ], Y[0:HD, 4:8, SEQ + 8 * b:SEQ + 8 * b + 8], ACT.Copy)
                act.activation(QBD[HD:P, s, :, DEC_SEQ:2 * DEC_SEQ], Y[HD:P, 4:8, SEQ + 8 * b:SEQ + 8 * b + 8],
                               ACT.Copy).then_inc(qbd_ready, 1)

            act.wait_ge(qbd_zero, 1)
            q_block_diag(0)
            for b in range(DEC_BATCH):
                if b + 1 < DEC_BATCH:
                    q_block_diag(b + 1)
                act.wait_ge(ss_max, b + 1)
                act.activation(SMS[:, :], SMS[:, :], ACT.Exp, bias=NM[:, 0, 0:1], accum_out=SUM[:, 0, 0:1])\
                   .then_inc(ss_exp, 1)
                for e, nb in enumerate((4, 4, 2)):
                    n = 3 * b + e
                    act.wait_ge(pts_mm, n + 1)
                    pb = PS[:, 5 + n % 2, :].rearrange("p (b f) -> p b f", f=P)
                    ins = act.activation(PTS[:, 4 * e:4 * e + nb, :], pb[:, 0:nb, :], ACT.Copy)
                    if e == 2:
                        ins = act.activation(PTS[0:NS, NB_D, :], pb[0:NS, 2, :], ACT.Copy)
                    ins.then_inc(pts_evac, 1)
            act.wait_ge(os_evac, DEC_BATCH)
            split_high(2, Y)
            mlp(1, "cache_d_v", "d_vs")
            for phase in (3, 4):
                for j in range(4):
                    ln_weave(3, phase, j)

        @block.vector
        def _(dve):
            links = [0]


            def link(ins):
                links[0] += 1
                ins.then_inc(dve_link, 1)
                dve.wait_ge(dve_link, links[0])

            def split_low(stage, src):
                for g, (c0, gw) in enumerate(GROUP):
                    dve.wait_ge(x_hi, 3 * stage + g + 1)
                    dve.tensor_tensor(XS[:, 1, :, c0:c0 + gw], src[:, :, c0:c0 + gw],
                                      XS[:, 0, :, c0:c0 + gw].bitcast(F32), ALU.subtract).then_inc(x_split, 1)

            def ln_weave(l, phase, quarter):
                if 0 <= phase - 2 <= 2 and quarter < 2 and l < 3:
                    g = phase - 2
                    c0, gw = GROUP[g]
                    for k in range(4 * quarter, 4 * quarter + 4):
                        n = 24 * l + 8 * g + k
                        dve.wait_ge(b_hi, n + 1)
                        xk = X[:, k, c0:c0 + gw]
                        dve.tensor_tensor(XS[:, 1, k, c0:c0 + gw], xk, XS[:, 0, k, c0:c0 + gw].bitcast(F32),
                                          ALU.subtract).then_inc(x_split, 1)
                        dve.wait_ge(x_split, XS_LN[l] + 8 * g + k + 1)
                        dve.tensor_scalar(xk, xk, ALPHA, None, ALU.mult).then_inc(x_scaled, 1)
                if 0 <= phase - 1 <= 2 and quarter > 0:
                    g, tt = phase - 1, quarter - 1
                    n = 9 * l + 3 * g + tt
                    r = tile_rows(3 * g + tt)
                    dve.wait_ge(ft_mm, n + 1)
                    dve.bn_stats(BNS[0:r, 0:6], FT[0:r, 0:512])
                    link(dve.bn_stats(BNS[0:r, 6:12], FT[0:r, 512:1024]))
                    link(dve.bn_aggr(MV[0:r, :], BNS[0:r, :]))
                    dve.tensor_scalar(VE[0:r, :], MV[0:r, 1:2], EPS, None, ALU.add).then_inc(ve_ready, 1)
                    dve.wait_ge(std_ready, n + 1)
                    link(dve.reciprocal(RS[0:r, :], SD[0:r, :]))
                    link(dve.scalar_tensor_tensor(out=NW[0:r, :], in0=RS[0:r, :], scalar=VE[0:r, :], in1=RS[0:r, :],
                                                  op0=ALU.mult, op1=ALU.mult))
                    link(dve.tensor_scalar(NW[0:r, :], NW[0:r, :], -0.5, 1.5, ALU.mult, ALU.add))
                    link(dve.tensor_tensor(RS[0:r, :], RS[0:r, :], NW[0:r, :], ALU.mult))
                    if n >= 3:
                        dve.wait_ge(bt_mm, 24 * l + 8 * g)
                    dve.tensor_scalar(ZN[0:r, tt, :], FT[0:r, :], MV[0:r, 0:1], RS[0:r, 0:1],
                                      ALU.subtract, ALU.mult).then_inc(zn_ready, 1)

            def taken(u):
                return bank(6 + u % 2)

            dve.wait_ge(cols_in, 64)
            dve.wait_ge(states_in, 16 * 8)
            split_low(0, X)
            dve.wait_ge(x_split, 3)
            link(dve.memset(CB[:, 0:2], 0.0))

            def ein_evac(t, g, u):
                c0, gw = GROUP[g]
                ps = taken(u)[:, 0:gw]
                bias = col(C_EBIN + t)
                pw = gw - (NS if g == 2 else 0)
                dve.wait_ge(p_mm, u + 1)
                if t == 0:
                    dve.tensor_scalar(KTA[:, c0:c0 + gw], ps, bias, None, ALU.add).then_inc(p_evac, 1)
                elif t == 1:
                    if g >= 2:
                        dve.wait_ge(vt_mm, g - 1)
                    dve.tensor_scalar(VT0[:, g % 2, 0:gw], ps, bias, None, ALU.add).then_inc(p_evac, 1)
                elif t < 6:
                    dve.tensor_scalar(Y[:, t - 2, c0:c0 + gw], ps, bias, QSCALE, ALU.add, ALU.mult).then_inc(p_evac, 1)
                else:
                    j, kind = divmod(t - 6, 3)
                    if kind == 0:
                        dve.tensor_scalar(HT[:, c0:c0 + gw], ps, bias, None, ALU.add).then_inc(p_evac, 1)
                        dve.wait_ge(p_evac, u + 1)
                    elif kind == 1:
                        link(dve.scalar_tensor_tensor(out=CB[:, 2 + c0:2 + c0 + pw], in0=ps[:, 0:pw], scalar=bias,
                                                      in1=HT[:, c0:c0 + pw], op0=ALU.add, op1=ALU.mult))
                        parts = [(CV[:, c0:c0 + pw], [CB[:, c0 + i:c0 + i + pw] for i in range(CONV_W)])]
                        if g == 2:
                            link(dve.scalar_tensor_tensor(
                                out=CS[:, j, :, 2:], in0=ps[:, pw:gw].rearrange("p (b i) -> p b i", b=DEC_BATCH), scalar=bias,
                                in1=HT[:, SEQ:NT].rearrange("p (b i) -> p b i", b=DEC_BATCH), op0=ALU.add, op1=ALU.mult))
                            parts.append((CV[:, SEQ:NT].rearrange("p (b i) -> p b i", b=DEC_BATCH),
                                          [CS[:, j, :, i:i + DEC_SEQ] for i in range(CONV_W)]))
                            dve.tensor_copy(BCO[:, j, :], CB[:, SEQ:SEQ + 2]).then_inc(bco_ready, 1)
                        for out, taps in parts:
                            link(dve.tensor_scalar(out, taps[0], col(C_CONV + j), None, ALU.mult))
                            for i in (1, 2):
                                ins = dve.scalar_tensor_tensor(out=out, in0=taps[i], scalar=col(C_CONV + 4 * i + j),
                                                               in1=out, op0=ALU.mult, op1=ALU.add)
                                if i == 1 or out is not parts[-1][0]:
                                    link(ins)
                        ins.then_inc(p_evac, 1)
                        dve.wait_ge(p_evac, u + 1)
                    else:
                        dve.scalar_tensor_tensor(out=Y[:, 4 + j, c0:c0 + gw], in0=ps, scalar=bias,
                                                 in1=CV[:, c0:c0 + gw], op0=ALU.add, op1=ALU.mult).then_inc(p_evac, 1)

            def a_scores(n):
                w, nk, k0 = job_a(n)
                half = n % 2
                sample = n == N_JOBS_A - 1
                if n == 0:
                    dve.wait_ge(biasa_in, 16)
                    dve.wait_ge(vt_mm, 3)
                if sample:
                    dve.wait_ge(bas_in, 16)
                dve.wait_ge(sa_mm, n + 1)
                s = PS[:, 0:2, :].rearrange("p a (b f) -> p (a b) f", f=256)
                for c in range(4):
                    bias = BAS[:, c, :] if sample else BA[:, half, c, 256 - w:256]
                    sink = SINK[:, 8 + c:9 + c] if sample else SINK[:, 4 * half + c:4 * half + c + 1]
                    ins = dve.tensor_tensor_reduce(out=SMA[:, c, 0:w], in0=s[:, c, 0:w], in1=bias, scale=1.0,
                                                   scalar=sink, op0=ALU.add, op1=ALU.max,
                                                   accum_out=MX[:, 0, c:c + 1])
                link(ins)
                link(dve.tensor_scalar(NM[:, 0, :], MX[:, 0, :], -1.0, None, ALU.mult))
                sinks = SINK[:, 8:12] if sample else SINK[:, 4 * half:4 * half + 4]
                dve.tensor_tensor(DS[:, :], sinks, NM[:, 0, :], ALU.add).then_inc(sa_max, 1)

            def a_output(n):
                dve.wait_ge(sa_exp, n + 1)
                link(dve.tensor_tensor(SUM[:, 0, :], SUM[:, 0, :], ES[:, :], ALU.add))
                link(dve.reciprocal(RD[:, 0, :], SUM[:, 0, :]))
                dve.wait_ge(oa_mm, n + 1)
                o = PS[:, 4, 0:256].rearrange("p (c f) -> p c f", c=4)
                half = n % 2
                if n < N_JOBS_A - 1:
                    dve.tensor_tensor(OTA[:, :, half * HD:half * HD + HD], o,
                                      RD[:, 0, :].unsqueeze(2).to_broadcast([P, 4, HD]), ALU.mult).then_inc(oa_evac, 1)
                else:
                    for h in range(2):
                        ins = dve.tensor_tensor(OTA[:, 0:2, h * HD:h * HD + HD], o[:, 2 * h:2 * h + 2, :],
                                                RD[:, 0, 2 * h:2 * h + 2].unsqueeze(2).to_broadcast([P, 2, HD]), ALU.mult)
                    ins.then_inc(oa_evac, 1)

            for s in range(4):
                for g in range(3):
                    for j in range(4):
                        u = 12 * s + 4 * g + j
                        ein_evac(4 * s + j, g, u)
                        if u == 23:
                            dve.wait_ge(p_evac, 24)
                            dve.tensor_copy(QS[:, :, :, :], Y[:, 0:4, SEQ:NT].rearrange("p c (b i) -> p b c i", b=DEC_BATCH))\
                               .then_inc(qs_ready, 1)
                        if s >= 2:
                            v = u - 24
                            if v % 2 == 0:
                                if v:
                                    a_output(v // 2 - 1)
                                a_scores(v // 2)
            for g in range(3):
                for j in range(2):
                    u = 48 + 2 * g + j
                    ein_evac(16 + j, g, u)
                    v = u - 24
                    if v % 2 == 0:
                        a_output(v // 2 - 1)
                        a_scores(v // 2)
            for n in range(15, N_JOBS_A):
                a_output(n - 1)
                a_scores(n)
            a_output(N_JOBS_A - 1)
            split_low(1, Y)

            def out_super(l, s):
                base = U_EOUT if l == 0 else U_OOUT
                for g, (c0, gw) in enumerate(GROUP):
                    for j in range(4):
                        u = base + 12 * s + 4 * g + j
                        m = 4 * s + j
                        if s == 0 and j == 0:
                            dve.wait_ge(xr_in[l][g], 16)
                            if l == 0:
                                link(dve.tensor_scalar(X[:, :, c0:c0 + gw], X[:, :, c0:c0 + gw], ALPHA, None, ALU.mult))
                        dve.wait_ge(p_mm, u + 1)
                        bias = col((C_EBOUT if l == 0 else C_OBOUT) + m)
                        dve.scalar_tensor_tensor(out=X[:, m, c0:c0 + gw], in0=taken(u)[:, 0:gw], scalar=bias,
                                                 in1=X[:, m, c0:c0 + gw], op0=ALU.add, op1=ALU.add).then_inc(p_evac, 1)
                        if s == 1:
                            ln_weave(2 * l, g, j)

            def hidden_low(l, i, weave):
                for g, (c0, gw) in enumerate(GROUP):
                    for j in range(4):
                        u = 4 * g + j
                        dve.wait_ge(hid_hi, 12 * i + (H_UNITS * l + u + 1))
                        dve.tensor_tensor(HID[:, 1, j, c0:c0 + gw], ST[:, u % 2, 0:gw],
                                          HID[:, 0, j, c0:c0 + gw].bitcast(F32), ALU.subtract).then_inc(hid_ready, 1)
                        if weave is not None and g < 2:
                            ln_weave(weave, 3 + g, j)

            def down_super(l, i, weave):
                for g, (c0, gw) in enumerate(GROUP):
                    for m in range(8):
                        v = 8 * g + m
                        dve.wait_ge(p_mm, 24 * i + (U_MLP[l] + v + 1))
                        dve.tensor_tensor(X[:, m, c0:c0 + gw], X[:, m, c0:c0 + gw], taken(v)[:, 0:gw],
                                          ALU.add).then_inc(p_evac, 1)
                        if weave is not None and m % 2 == 1:
                            ln_weave(weave, g, m // 2)

            def mlp(l):
                hidden_low(l, 0, 2 * l)
                dve.wait_ge(x_scaled, 48 * l + 24)
                with dve.Fori(0, N_HB - 1) as i:
                    down_super(l, i, None)
                    hidden_low(l, i + 1, None)
                down_super(l, N_HB - 1, 2 * l + 1)

            for s in range(2):
                out_super(0, s)
            mlp(0)

            def oin_evac(s, g, j, u):
                c0, gw = GROUP[g]
                ps = taken(u)[:, 0:gw]
                bias = col(C_OBIN + 4 * s + j)
                dve.wait_ge(p_mm, u + 1)
                if s == 0:
                    dve.tensor_scalar(Y[:, 4 + j, c0:c0 + gw], ps, bias, QSCALE, ALU.add, ALU.mult).then_inc(p_evac, 1)
                elif s == 1:
                    if g == 2:
                        dve.tensor_scalar(US[:, j, :, POOL_HIST:],
                                          ps[:, gw - NS:gw].rearrange("p (b i) -> p b i", b=DEC_BATCH), bias, None, ALU.add)
                        gw -= NS
                    dve.tensor_scalar(Y[:, j, c0:c0 + gw], ps[:, 0:gw], bias, None, ALU.add).then_inc(p_evac, 1)
                elif s == 2:
                    if g == 0 and j == 0:
                        dve.wait_ge(spilled, 48)
                    dve.tensor_scalar(KTD[:, j, c0:c0 + gw], ps, bias, None, ALU.add).then_inc(p_evac, 1)
                else:
                    dve.tensor_scalar(VT1[:, (4 * g + j) % 2, 0:gw], ps, bias, None, ALU.add).then_inc(p_evac, 1)

            def pooled(c):
                w = POOL_WINDOWS[c]
                if c:
                    dve.wait_ge(p_mm, U_OIN + 36 + 7 * c)
                u, src, dst, step = Y[:, c, 0:SEQ], PA, PB, 2
                dve.tensor_copy(UO[:, c, :], Y[:, c, SEQ - POOL_HIST:SEQ]).then_inc(uo_ready, 1)
                dve.tensor_copy(PA[:, 16:17], u[:, 0:1])
                link(dve.tensor_tensor(PA[:, 17:16 + SEQ], u[:, 1:SEQ], u[:, 0:SEQ - 1], ALU.add))
                while step < w:
                    link(dve.tensor_tensor(dst[:, 16:16 + SEQ], src[:, 16:16 + SEQ], src[:, 16 - step:16 - step + SEQ], ALU.add))
                    src, dst, step = dst, src, 2 * step
                link(dve.scalar_tensor_tensor(out=PO[:, 0:SEQ], in0=src[:, 16:16 + SEQ], scalar=1.0 / w, in1=u,
                                              op0=ALU.mult, op1=ALU.subtract))
                link(dve.tensor_tensor(PO[:, 0:16], src[:, 16:32], RC[:, c, :], ALU.mult))
                link(dve.tensor_tensor(PO[:, 0:16], PO[:, 0:16], u[:, 0:16], ALU.subtract))
                us, src, dst, step, lo = US[:, c, :, :], SA, SB, 2, 1
                link(dve.tensor_tensor(SA[:, :, 1:], us[:, :, 1:], us[:, :, :-1], ALU.add))
                while step < w:
                    lo += step
                    link(dve.tensor_tensor(dst[:, :, lo:], src[:, :, lo:], src[:, :, lo - step:23 - step], ALU.add))
                    src, dst, step = dst, src, 2 * step
                dve.scalar_tensor_tensor(out=PO[:, SEQ:NT].rearrange("p (b i) -> p b i", b=DEC_BATCH),
                                         in0=src[:, :, POOL_HIST:], scalar=1.0 / w, in1=us[:, :, POOL_HIST:],
                                         op0=ALU.mult, op1=ALU.subtract).then_inc(po_ready, 1)

            def group_evac(c, u0):
                for g, (c0, gw) in enumerate(GROUP):
                    dve.wait_ge(p_mm, u0 + g + 1)
                    dve.tensor_scalar(Y[:, c, c0:c0 + gw], taken(u0 + g)[:, 0:gw], col(C_CSCALE + c), None, ALU.mult)\
                       .then_inc(p_evac, 1)

            for s in range(3):
                for g in range(3):
                    for j in range(4):
                        oin_evac(s, g, j, U_OIN + 12 * s + 4 * g + j)
                        if s == 0 and g < 2:
                            ln_weave(1, 3 + g, j)
            dve.memset(PA[:, 0:16], 0.0)
            link(dve.memset(PB[:, 0:16], 0.0))
            for g in range(3):
                for j in range(4):
                    oin_evac(3, g, j, U_OIN + 36 + 7 * g + j)
                    if j == 1:
                        pooled(g)
                group_evac(g, U_OIN + 36 + 7 * g + 4)
            pooled(3)
            group_evac(3, U_OIN + 57)

            def d_scores(m):
                h, qb = divmod(m, 8)
                w = P * (qb + 1)
                if qb == 0:
                    dve.wait_ge(th_in[h % 2], 16 * (h // 2 + 1))
                dve.wait_ge(sd_mm, m + 1)
                s = PS[:, 2 * (m % 2):2 * (m % 2) + 2, :].rearrange("p a b -> p (a b)")
                link(dve.tensor_tensor_reduce(out=SMD[:, m % 2, 0:w], in0=s[:, 0:w], in1=TH[:, h % 2, SEQ - w:SEQ],
                                              scale=1.0, scalar=NEG, op0=ALU.add, op1=ALU.max,
                                              accum_out=MX[:, m % 2, 0:1]))
                dve.tensor_scalar(NM[:, m % 2, 0:1], MX[:, m % 2, 0:1], -1.0, None, ALU.mult).then_inc(sd_max, 1)

            def d_output(m):
                h, qb = divmod(m, 8)
                dve.wait_ge(sd_exp, m + 1)
                link(dve.reciprocal(RD[:, m % 2, 0:1], SUM[:, m % 2, 0:1]))
                dve.wait_ge(od_mm, m + 1)
                if m % 16 == 0 and m:
                    dve.wait_ge(ptd_mm, piece_base[m])
                dve.tensor_scalar(OTD[:, qb, (h % 2) * HD:(h % 2) * HD + HD], PS[:, 6 + m % 2, 0:HD],
                                  RD[:, m % 2, 0:1], None, ALU.mult).then_inc(od_evac, 1)

            d_scores(0)
            for m in range(64):
                if m + 1 < 64:
                    d_scores(m + 1)
                d_output(m)
            dve.wait_ge(ptd_evac, piece_base[64])
            dve.memset(QBD[:, :, :, :], 0.0).then_inc(qbd_zero, 1)
            dve.wait_ge(bs_in, 32)

            def ktc_take(b):
                for c in range(4):
                    for e, nb in enumerate((4, 4, 2)):
                        n = 12 * b + 3 * c + e
                        dve.wait_ge(ktc_mm, n + 1)
                        dve.tensor_copy(KTC[:, c % 2, 512 * e:512 * e + nb * P], bank(3 + n % 2, nb * P)).then_inc(ktc_evac, 1)

            ktc_take(0)
            for b in range(DEC_BATCH):
                link(dve.tensor_copy(BS[:, NB_D * P:], BNEW[:, b, :]))
                dve.wait_ge(ss_mm, b + 1)
                if b:
                    dve.wait_ge(pts_mm, 3 * b)
                link(dve.tensor_tensor_reduce(out=SMS[:, :], in0=PS[:, 0:3, :].rearrange("p a b -> p (a b)")[:, 0:KEYS_D],
                                              in1=BS[:, :], scale=1.0, scalar=NEG, op0=ALU.add, op1=ALU.max,
                                              accum_out=MX[:, 0, 0:1]))
                dve.tensor_scalar(NM[:, 0, 0:1], MX[:, 0, 0:1], -1.0, None, ALU.mult).then_inc(ss_max, 1)
                dve.wait_ge(ss_exp, b + 1)
                link(dve.reciprocal(RD[:, 0, 0:1], SUM[:, 0, 0:1]))
                dve.tensor_scalar(SMS[:, :], SMS[:, :], RD[:, 0, 0:1], None, ALU.mult).then_inc(ss_prob, 1)
                if b + 1 < DEC_BATCH:
                    ktc_take(b + 1)
                dve.wait_ge(os_mm, b + 1)
                o = PS[:, 7, 0:P].rearrange("p (c r) -> p c r", c=4)
                dve.tensor_copy(Y[0:HD, 4:8, SEQ + 8 * b:SEQ + 8 * b + 8], o[0:HD, :, 0:DEC_SEQ])
                dve.tensor_copy(Y[HD:P, 4:8, SEQ + 8 * b:SEQ + 8 * b + 8], o[HD:P, :, DEC_SEQ:2 * DEC_SEQ]).then_inc(os_evac, 1)
            split_low(2, Y)
            for s in range(2):
                out_super(1, s)
            mlp(1)
            for phase in (3, 4):
                for j in range(4):
                    ln_weave(3, phase, j)

        @block.tensor
        def _(pe):
            def product(out, slot, off, nk, src, g, done):
                c0, gw = GROUP[g]
                n = 0
                for k in range(nk):
                    for a, b in ((0, 0), (1, 0), (0, 1)):
                        last = pe.matmul(out[:, 0:gw], WS[:, slot, a, (off + k) * P:(off + k + 1) * P],
                                         src[:, b, k, c0:c0 + gw], start=(n == 0), stop=(n == 3 * nk - 1))
                        n += 1
                last.then_inc(done, 1)

            def unit(u, t, g):
                if g == 0:
                    pe.wait_ge(w_split, t + 1)
                if u >= 2:
                    pe.wait_ge(p_evac, u - 1)
                product(bank(6 + u % 2), t % NSLOT, 0, KC, XS, g, p_mm)

            def ln_weave(l, phase, quarter, group_done):
                if 0 <= phase - 2 <= 2 and quarter < 2:
                    g = phase - 2
                    for k in range(4 * quarter, 4 * quarter + 4):
                        n = 24 * l + 8 * g + k
                        if k == 0:
                            pe.wait_ge(zn_ready, 9 * l + 3 * g + 3)
                        if n >= 2:
                            pe.wait_ge(b_evac, n - 1)
                        for tt in range(3):
                            r = tile_rows(3 * g + tt)
                            last = pe.transpose(PS[:, 2 + n % 2, tt * P:tt * P + r], ZN[0:r, tt, k * P:k * P + P],
                                                IDN[0:r, 0:r])
                        last.then_inc(bt_mm, 1)
                if 0 <= phase - 1 <= 2 and quarter > 0:
                    g, tt = phase - 1, quarter - 1
                    t = 3 * g + tt
                    r = tile_rows(t)
                    if tt == 0:
                        pe.wait_ge(p_evac, group_done[g])
                    if 9 * l + t:
                        pe.wait_ge(zn_ready, 9 * l + t)
                    for k in range(KC):
                        last = pe.transpose(FT[0:r, k * P:k * P + P], X[:, k, t * P:t * P + r], IDN[:, :])
                    last.then_inc(ft_mm, 1)

            def v_transpose(n, src, gw):
                if n >= 2:
                    pe.wait_ge(vt_evac, n - 1)
                for tt in range(3):
                    r = min(P, gw - tt * P)
                    last = pe.transpose(PS[0:r, 4 + n % 2, tt * P:tt * P + P], src[:, tt * P:tt * P + r], IDN[:, :])
                last.then_inc(vt_mm, 1)

            pe.wait_ge(ident_in, 16)
            pe.wait_ge(kca_in, 16)
            for h in range(2):
                for b in range(4):
                    last = pe.transpose(PS[:, 2 + h, b * P:b * P + P], KCA[:, 4 * h + b, :], IDN[:, :])
                last.then_inc(kct_mm, 1)
            for s in range(2):
                for g in range(3):
                    if s == 0:
                        pe.wait_ge(x_split, g + 1)
                    for j in range(4):
                        unit(12 * s + 4 * g + j, 4 * s + j, g)
                        if s == 0 and j == 2:
                            pe.wait_ge(p_evac, 4 * g + 2)
                            v_transpose(g, VT0[:, g % 2, :], GROUP[g][1])
            pe.wait_ge(vt_evac, 3)
            pe.transpose(PS[0:NS, 4, 0:P], KTA[:, SEQ:NT], IDN[:, :]).then_inc(kn_mm, 1)

            def a_scores(n):
                w, nk, k0 = job_a(n)
                qb, half = divmod(n, 2)
                lo = half * HD
                if n:
                    pe.wait_ge(sa_max, n)
                else:
                    pe.wait_ge(p_evac, 24)
                s = PS[:, 0:2, :].rearrange("p a (b f) -> p (a b) f", f=256)
                if n < N_JOBS_A - 1:
                    for c in range(4):
                        last = pe.matmul(s[:, c, 0:w], Y[lo:lo + HD, c, qb * P:qb * P + P],
                                         KTA[lo:lo + HD, k0:k0 + w], start=True, stop=True)
                else:
                    pe.wait_ge(kct_evac, 2)
                    pe.wait_ge(qs_ready, 1)
                    for half in range(2):
                        lo = half * HD
                        for b in range(DEC_BATCH):
                            rows = 32 * (b % 4)
                            q = QS[lo:lo + HD, b, :, :].rearrange("p c i -> p (c i)")
                            o = s[rows:rows + 32, 2 * half + b // 4, :]
                            pe.matmul(o[:, 0:P], q, KCT[lo:lo + HD, b, :], start=True, stop=True)
                            last = pe.matmul(o[:, P:192], q, KTA[lo:lo + HD, SEQ:NT], start=True, stop=True)
                last.then_inc(sa_mm, 1)

            def a_transpose(n):
                w, nk, k0 = job_a(n)
                pe.wait_ge(sa_exp, n + 1)
                if n:
                    pe.wait_ge(pta_evac, n)
                o = PS[:, 2:4, :].rearrange("p a (b f) -> p (a b) f", f=P)
                if n < N_JOBS_A - 1:
                    for c in range(4):
                        for kb in range(nk):
                            last = pe.transpose(o[:, nk * c + kb, :], SMA[:, c, kb * P:kb * P + P], IDN[:, :])
                else:
                    for i in range(4):
                        pe.transpose(o[:, i, :], SMA[:, i, 0:P], IDN[:, :])
                        last = pe.transpose(o[0:NS, 4 + i, :], SMA[:, i, P:192], IDN[:, :])
                last.then_inc(pta_mm, 1)

            def a_values(n):
                w, nk, k0 = job_a(n)
                qb, half = divmod(n, 2)
                pe.wait_ge(pta_evac, n + 1)
                if n:
                    pe.wait_ge(oa_evac, n)
                else:
                    pe.wait_ge(kn_evac, 1)
                o = PS[:, 4, 0:256].rearrange("p (c f) -> p c f", c=4)
                if n < N_JOBS_A - 1:
                    for c in range(4):
                        for kb in range(nk):
                            last = pe.matmul(o[:, c, :], PTA[:, nk * c + kb, :],
                                             VA[:, k0 // P + kb, half * HD:half * HD + HD],
                                             start=(kb == 0), stop=(kb == nk - 1))
                else:
                    pe.wait_ge(vca_in, 16)
                    for half in range(2):
                        hd = slice(half * HD, half * HD + HD)
                        for b in range(DEC_BATCH):
                            rows = slice(32 * (b % 4), 32 * (b % 4) + 32)
                            i = 2 * half + b // 4
                            pe.matmul(o[rows, i, :], PTA[:, i, rows], VCA[:, b, hd], start=True, stop=False)
                            last = pe.matmul(o[rows, i, :], PTA[0:NS, 4 + i, rows], VA[0:NS, 8, hd],
                                             start=False, stop=True)
                last.then_inc(oa_mm, 1)

            def a_out(qb):
                pe.wait_ge(oa_evac, 2 * qb + 2)
                if qb:
                    pe.wait_ge(ota_evac, qb)
                for c in range(4):
                    last = pe.transpose(PS[:, 5, c * P:c * P + P], OTA[:, c, :], IDN[:, :])
                last.then_inc(ota_mm, 1)

            def a_slot(v):
                n = v // 2
                if v % 2 == 0:
                    if n:
                        a_values(n - 1)
                    a_scores(n)
                else:
                    a_transpose(n)
                    if n >= 2 and n % 2 == 0:
                        a_out(n // 2 - 1)

            for s in range(2, 4):
                for g in range(3):
                    for j in range(4):
                        unit(12 * s + 4 * g + j, 4 * s + j, g)
                        a_slot(12 * (s - 2) + 4 * g + j)
            for g in range(3):
                for j in range(2):
                    unit(48 + 2 * g + j, 16 + j, g)
                    a_slot(24 + 2 * g + j)
            for n in range(15, N_JOBS_A):
                a_slot(2 * n)
                a_slot(2 * n + 1)
            a_values(N_JOBS_A - 1)
            pe.wait_ge(oa_evac, N_JOBS_A)
            pe.wait_ge(ota_evac, 8)
            for quad in range(2):
                last = pe.transpose(PS[:, 5, quad * P:quad * P + P], OTA[:, quad, :], IDN[:, :])
            last.then_inc(ota_mm, 1)

            def out_projection(l, t0, u0, xs):
                done = [u0 + 12 + 4 * g + 4 for g in range(3)]
                for s in range(2):
                    for g in range(3):
                        if s == 0:
                            pe.wait_ge(x_split, xs + g + 1)
                        for j in range(4):
                            unit(u0 + 12 * s + 4 * g + j, t0 + 4 * s + j, g)
                            if s == 1:
                                ln_weave(2 * l, g, j, done)
                return done

            def hidden_super(l, i, weave, done):
                t0 = T_MLP[l]
                for g in range(3):
                    if weave is not None:
                        pe.wait_ge(x_split, XS_LN[2 * l] + 8 * (g + 1))
                    for j in range(4):
                        u = 4 * g + j
                        n = 12 * i + (H_UNITS * l + u)
                        if g == 0:
                            pe.wait_ge(w_split, 8 * i + (t0 + j + 1))
                        if not (isinstance(n, int) and n < 2):
                            pe.wait_ge(h_evac, n - 1)
                        product(bank(4 + u % 2), (t0 + j) % NSLOT, 0, KC, XS, g, h_mm)
                        if weave is not None and g < 2:
                            ln_weave(weave, 3 + g, j, done)

            def down_super(l, i, weave):
                t0 = T_MLP[l] + 4
                done = [U_MLP[l] + 24 * (N_HB - 1) + 8 * g + 8 for g in range(3)]
                for g in range(3):
                    pe.wait_ge(hid_ready, 12 * i + (H_UNITS * l + 4 * g + 4))
                    for j in range(4):
                        if g == 0:
                            pe.wait_ge(w_split, 8 * i + (t0 + j + 1))
                        for mm in range(2):
                            v = 8 * g + 2 * j + mm
                            pe.wait_ge(p_evac, 24 * i + (U_MLP[l] + v - 1))
                            product(bank(6 + v % 2), (t0 + j) % NSLOT, 4 * mm, 4, HID, g, p_mm)
                        if weave is not None:
                            ln_weave(weave, g, j, done)
                return done

            def mlp(l, done):
                hidden_super(l, 0, 2 * l, done)
                with pe.Fori(0, N_HB - 1) as i:
                    down_super(l, i, None)
                    hidden_super(l, i + 1, None, None)
                return down_super(l, N_HB - 1, 2 * l + 1)

            pe.wait_ge(ota_evac, 10)
            done = mlp(0, out_projection(0, T_EOUT, U_EOUT, XS_MIX0))

            def group_product(c, u0):
                pe.wait_ge(po_ready, c + 1)
                for g, (c0, gw) in enumerate(GROUP):
                    pe.wait_ge(p_evac, u0 + g - 1)
                    pe.matmul(bank(6 + (u0 + g) % 2, gw), GW[:, c, :], PO[:, c0:c0 + gw],
                              start=True, stop=True).then_inc(p_mm, 1)

            for s in range(4):
                for g in range(3):
                    if s == 0:
                        pe.wait_ge(x_split, XS_LN1 + 8 * (g + 1))
                    for j in range(4):
                        n = 4 * g + j
                        unit(U_OIN + 12 * s + (4 if s < 3 else 7) * g + j, T_OIN + 4 * s + j, g)
                        if s == 0 and g < 2:
                            ln_weave(1, 3 + g, j, done)
                        if s == 3 and n:
                            pg, pj = divmod(n - 1, 4)
                            pe.wait_ge(p_evac, U_OIN + 36 + 7 * pg + pj + 1)
                            v_transpose(3 + n - 1, VT1[:, (n - 1) % 2, :], GROUP[pg][1])
                    if s == 3:
                        group_product(g, U_OIN + 36 + 7 * g + 4)
                if s == 2:
                    pe.wait_ge(p_evac, U_OIN + 36)
                    pe.wait_ge(b_evac, 48)
                    for c in range(4):
                        last = pe.transpose(PS[0:NS, 3, c * P:c * P + P], KTD[:, c, SEQ:NT], IDN[:, :])
                    last.then_inc(kn_mm, 1)
            pe.wait_ge(p_evac, U_OIN + 54)
            v_transpose(14, VT1[:, 1, :], GROUP[2][1])
            group_product(3, U_OIN + 57)

            def d_scores(m):
                h, qb = divmod(m, 8)
                w = P * (qb + 1)
                lo = (h % 2) * HD
                if m >= 2:
                    pe.wait_ge(sd_max, m - 1)
                for k0 in range(0, w, 512):
                    kw = min(512, w - k0)
                    last = pe.matmul(bank(2 * (m % 2) + k0 // 512, kw), Y[lo:lo + HD, 4 + h // 2, qb * P:qb * P + P],
                                     KTD[lo:lo + HD, h // 2, k0:k0 + kw], start=True, stop=True)
                last.then_inc(sd_mm, 1)

            def d_transpose(m):
                pe.wait_ge(sd_exp, m + 1)
                for e, (k, nk) in enumerate(pieces_d(m)):
                    n = piece_base[m] + e
                    if n >= 2:
                        pe.wait_ge(ptd_evac, n - 1)
                    for kb in range(nk):
                        last = pe.transpose(PS[:, 4 + n % 2, kb * P:kb * P + P], SMD[:, m % 2, (k + kb) * P:(k + kb + 1) * P],
                                            IDN[:, :])
                    last.then_inc(ptd_mm, 1)

            def d_values(m):
                h, qb = divmod(m, 8)
                pe.wait_ge(ptd_evac, piece_base[m] + len(pieces_d(m)))
                if m >= 2:
                    pe.wait_ge(od_evac, m - 1)
                for kb in range(qb + 1):
                    last = pe.matmul(PS[:, 6 + m % 2, 0:HD], PTD[:, m % 2, kb, :], VD[:, kb, h * HD:h * HD + HD],
                                     start=(kb == 0), stop=(kb == qb))
                last.then_inc(od_mm, 1)

            pe.wait_ge(p_evac, U_OOUT)
            pe.wait_ge(kn_evac, 2)
            pe.wait_ge(vt_evac, 15)
            d_scores(0)
            d_scores(1)
            for m in range(64):
                d_transpose(m)
                if m + 2 < 64:
                    d_scores(m + 2)
                d_values(m)
                if m % 16 == 15:
                    pe.wait_ge(od_evac, m + 1)
                    for e in range(2):
                        n = piece_base[m + 1] - 2 + e
                        pe.wait_ge(ptd_evac, n - 1)
                        for t in range(4):
                            last = pe.transpose(PS[:, 4 + n % 2, t * P:t * P + P], OTD[:, 4 * e + t, :], IDN[:, :])
                        last.then_inc(ptd_mm, 1)

            def s_keys(b, c):
                if c == 0:
                    pe.wait_ge(ks_in, 80 * (b + 1))
                for e, nb in enumerate((4, 4, 2)):
                    n = 12 * b + 3 * c + e
                    if n >= 2:
                        pe.wait_ge(ktc_evac, n - 1)
                    for i in range(nb):
                        last = pe.transpose(PS[:, 3 + n % 2, i * P:i * P + P], KCD[:, 4 * e + i, c * P:c * P + P], IDN[:, :])
                    last.then_inc(ktc_mm, 1)

            def s_scores(b, c):
                pe.wait_ge(ktc_evac, 12 * b + 3 * c + 3)
                if c == 0:
                    pe.wait_ge(qbd_ready, b + 1)
                    if b:
                        pe.wait_ge(ss_max, b)
                rows = slice(32 * c, 32 * c + 32)
                for e, nb in enumerate((4, 4, 2)):
                    pe.matmul(PS[rows, e, 0:nb * P], QBD[:, b % 2, c, :], KTC[:, c % 2, 512 * e:512 * e + nb * P],
                              start=True, stop=True)
                last = pe.matmul(PS[rows, 2, 2 * P:2 * P + NS], QBD[:, b % 2, c, :], KTD[:, c, SEQ:NT], start=True, stop=True)
                if c == 3:
                    last.then_inc(ss_mm, 1)

            def s_keys_scores(b):
                s_keys(b, 0)
                for c in range(4):
                    if c < 3:
                        s_keys(b, c + 1)
                    s_scores(b, c)

            pe.wait_ge(ptd_evac, piece_base[64])
            pe.wait_ge(od_evac, 64)
            s_keys_scores(0)
            for b in range(DEC_BATCH):
                if b + 1 < DEC_BATCH:
                    s_keys_scores(b + 1)
                pe.wait_ge(ss_prob, b + 1)
                for e, nb in enumerate((4, 4, 2)):
                    n = 3 * b + e
                    if n >= 2:
                        pe.wait_ge(pts_evac, n - 1)
                    for i in range(nb):
                        last = pe.transpose(PS[:, 5 + n % 2, i * P:i * P + P], SMS[:, (4 * e + i) * P:(4 * e + i + 1) * P],
                                            IDN[:, :])
                    if e == 2:
                        last = pe.transpose(PS[0:NS, 5 + n % 2, 2 * P:3 * P], SMS[:, NB_D * P:], IDN[:, :])
                    last.then_inc(pts_mm, 1)
                pe.wait_ge(pts_evac, 3 * b + 3)
                pe.wait_ge(vs_in, 80 * (b + 1))
                if b:
                    pe.wait_ge(os_evac, b)
                for c in range(4):
                    o = PS[:, 7, 32 * c:32 * c + 16]
                    for i in range(NB_D):
                        pe.matmul(o, VCD[:, i, c * P:c * P + P], PTS[:, i, 32 * c:32 * c + 16], start=(i == 0), stop=False)
                    last = pe.matmul(o, VN[:, c * P:c * P + P], PTS[0:NS, NB_D, 32 * c:32 * c + 16], start=False, stop=True)
                last.then_inc(os_mm, 1)
            pe.wait_ge(os_evac, DEC_BATCH)
            done = mlp(1, out_projection(1, T_OOUT, U_OOUT, XS_MIX1))
            for phase in (3, 4):
                for j in range(4):
                    ln_weave(3, phase, j, done)


def slopes(n):
    return 2.0 ** (-8.0 * np.arange(1, n + 1) / n)


def dilated(dist):
    n = sum(((dist >= 0) & (dist <= w) & (dist % d == 0)).astype(np.float64) for w, d in D_BRANCHES)
    return np.where(n > 0, np.log(np.maximum(n, 1)), NEG)


def tables():
    p = np.arange(P)
    sl = slopes(A_HEADS)
    t = {"ident": np.eye(P)}
    dist = P + p[:, None] - np.arange(2 * P)[None, :]
    ok = (dist >= 0) & (dist <= A_WINDOW)
    t["ba"] = np.stack([np.stack([np.where(ok, -sl[4 * half + c] * dist, NEG) for c in range(4)], 1)
                        for half in range(2)], 1)
    bb, c, i = p // 32, p % 32 // 8, p % 8
    sets = []
    for half in range(2):
        s = sl[4 * half + c][:, None]
        for quad in range(2):
            dist = A_WINDOW + i[:, None] - p[None, :]
            old = np.where((dist >= 0) & (dist <= A_WINDOW), -s * dist, NEG)
            nb, ni = np.arange(NS)[None, :] // 8, np.arange(NS)[None, :] % 8
            ok = (nb == 4 * quad + bb[:, None]) & (ni <= i[:, None])
            sets.append(np.concatenate([old, np.where(ok, -s * (i[:, None] - ni), NEG)], 1))
    t["bas"] = np.stack(sets, 1)
    dist = SEQ - P + p[:, None] - np.arange(SEQ)[None, :]
    t["th"] = np.stack([np.where(dist >= 0, -s * dist, 0) + dilated(dist) for s in slopes(D_HEADS)])
    c, hh, i = p // 32, p % 32 // 8, p % 8
    s = np.where(hh < 2, slopes(D_HEADS)[np.minimum(2 * c + hh, D_HEADS - 1)], 0)[:, None]
    live = (hh < 2)[:, None]
    rows = np.zeros((NB_D, P), int)
    for blk in range(8):
        rows[blk] = 16 * p + blk
    for e in range(2):
        rows[8 + e] = 16 * (96 + p % 32) + 8 + 2 * (p // 32) + e
    dist = D_WINDOW + i[:, None] - rows.reshape(-1)[None, :]
    t["bs"] = np.where(live, -s * dist + dilated(dist), 0)
    nb, ni = np.arange(NS)[None, :] // 8, np.arange(NS)[None, :] % 8
    d = i[:, None] - ni
    t["bnew"] = np.stack([np.where(live, np.where(nb == b, -s * d + dilated(d), NEG), 0) for b in range(DEC_BATCH)], 1)
    w = np.array(POOL_WINDOWS)[:, None]
    t["rc"] = np.broadcast_to(1.0 / np.minimum(np.arange(16)[None, :] + 1, w), (P, 4, 16))
    return {k: np.ascontiguousarray(v, dtype=np.float32) for k, v in t.items()}


def kernel(x_prompt, x_sample, cache_a_k, cache_a_v, state_b_conv, state_c_pool, cache_d_k, cache_d_v,
           even_w_in, even_b_in, a_sinks, b_conv_w, even_w_out, even_b_out,
           odd_w_in, odd_b_in, c_w_group, c_scale, odd_w_out, odd_b_out,
           mlp_w1, mlp_w2, ln1_g, ln1_b, ln2_g, ln2_b):
    import concourse.bacc as bacc
    from concourse.bass_utils import run_bass_kernel_spmd as run

    A = np.asarray
    B = DEC_BATCH

    def features(a):
        a = A(a).reshape(-1, a.shape[-1])
        return a.T.reshape(a.shape[1] // P, P, a.shape[0]).transpose(1, 0, 2)

    def in_tiles(w):
        w = A(w)
        n = w.shape[1] // P
        return w.reshape(KC, P, n, P).transpose(2, 1, 0, 3).reshape(n, P, 1024)

    def down_tiles(w):
        return A(w).reshape(4, P, 4, 2, P).transpose(2, 1, 3, 0, 4).reshape(4, P, 1024)

    pairs = np.arange(A_HEADS * HD).reshape(2, 4, HD).transpose(1, 0, 2).reshape(-1)
    e = np.arange(4 * P).reshape(4, P)
    order = np.concatenate([512 + np.arange(256), pairs] + [np.concatenate([768 + e[j], 1792 + e[j], 1280 + e[j]]) for j in range(4)])
    o = np.arange(512)
    oorder = np.concatenate([512 + o, o, 1024 + o, 1536 + o])
    w1, w2 = A(mlp_w1), A(mlp_w2)

    def mlp_tiles(l):
        return [t for h in range(N_HB) for t in (in_tiles(w1[l][:, 512 * h:512 * h + 512]),
                                                 down_tiles(w2[l][512 * h:512 * h + 512]))]

    w = np.concatenate([in_tiles(A(even_w_in)[0][:, order]),
                        in_tiles(A(even_w_out)[0][np.concatenate([pairs, 512 + o])])] + mlp_tiles(0)
                       + [in_tiles(A(odd_w_in)[0][:, oorder]), in_tiles(A(odd_w_out)[0])] + mlp_tiles(1))

    def columns(*vs):
        return [A(v).reshape(-1, P).T for v in vs]

    cols = np.concatenate(columns(A(even_b_in)[0][order], A(b_conv_w)[0], even_b_out, A(odd_b_in)[0][oorder], c_scale,
                                  odd_b_out, ln1_g[0], ln2_g[0], ln1_g[1], ln2_g[1],
                                  ln1_b[0], ln2_b[0], ln1_b[1], ln2_b[1]), 1)
    head = np.arange(P) % 32 // 8
    sinks = A(a_sinks)[0]
    sink = np.concatenate([np.broadcast_to(sinks, (P, 8)),
                           np.stack([sinks[head], sinks[head], sinks[head + 4], sinks[head + 4]], 1)], 1)
    ins = dict(tables())
    ins.update(
        x=np.concatenate([features(x_prompt), features(x_sample)], 2), w=w, cols=cols, sink=sink,
        gw=A(c_w_group)[0].transpose(1, 0, 2),
        b_state=features(state_b_conv).reshape(P, 4, B, 2), c_state=features(state_c_pool).reshape(P, 4, B, POOL_HIST),
        cache_a_k=A(cache_a_k).reshape(B, A_WINDOW, P), cache_a_v=A(cache_a_v).reshape(B, A_WINDOW, P),
        cache_d_k=A(cache_d_k).reshape(B, D_WINDOW, 512), cache_d_v=A(cache_d_v).reshape(B, D_WINDOW, 512))
    ins = {k: np.ascontiguousarray(v) for k, v in ins.items()}
    outs = dict(y=(P, KC, NT), a_k=(P, A_WINDOW), a_v=(A_WINDOW, P), b_c=(P, 4, 2), c_p=(P, 4, POOL_HIST),
                d_k=(P, 4, SEQ), d_v=(SEQ, 512), a_ks=(B, A_WINDOW, P), a_vs=(B, A_WINDOW, P),
                b_cs=(P, 4, B, 2), c_ps=(P, 4, B, POOL_HIST), d_ks=(B, D_WINDOW, 512), d_vs=(B, D_WINDOW, 512))

    nc = bacc.Bacc("TRN2", target_bir_lowering=False, num_devices=1)
    F32 = mybir.dt.float32
    io = {k: nc.dram_tensor("in_" + k, v.shape, F32, kind="ExternalInput").ap() for k, v in ins.items()}
    io.update({k: nc.dram_tensor("out_" + k, v, F32, kind="ExternalOutput").ap() for k, v in outs.items()})
    io["spill"] = nc.dram_tensor("spill", (P, KC, NT), F32, kind="Internal").ap()
    build(nc, io)
    r = run(nc, [{"in_" + k: v for k, v in ins.items()}], core_ids=[0]).results[0]
    r = {k: r["out_" + k] for k in outs}

    def tokens(a):
        return a.transpose(2, 1, 0).reshape(a.shape[2], -1)

    y = tokens(r["y"])
    return (y[:SEQ].reshape(1, SEQ, D_MODEL), y[SEQ:].reshape(B, DEC_SEQ, D_MODEL),
            r["a_k"].T.reshape(1, 1, A_WINDOW, 2, HD), r["a_v"].reshape(1, 1, A_WINDOW, 2, HD),
            tokens(r["b_c"]).reshape(1, 1, 2, B_WIDTH), tokens(r["c_p"]).reshape(1, 1, POOL_HIST, 512),
            tokens(r["d_k"]).reshape(1, 1, SEQ, 8, HD), r["d_v"].reshape(1, 1, SEQ, 8, HD),
            r["a_ks"].reshape(1, B, A_WINDOW, 2, HD), r["a_vs"].reshape(1, B, A_WINDOW, 2, HD),
            tokens(r["b_cs"].reshape(P, 4, B * 2)).reshape(1, B, 2, B_WIDTH),
            tokens(r["c_ps"].reshape(P, 4, B * POOL_HIST)).reshape(1, B, POOL_HIST, 512),
            r["d_ks"].reshape(1, B, D_WINDOW, 8, HD), r["d_vs"].reshape(1, B, D_WINDOW, 8, HD))
```

```python
import numpy as np
import concourse.bass as bass
from concourse import mybir
from contextlib import ExitStack

P = 128
D_MODEL, SEQ, DEC_BATCH, DEC_SEQ = 1024, 1024, 8, 8
NS = DEC_BATCH * DEC_SEQ
NT = SEQ + NS
KC = D_MODEL // P
HD = 64
A_HEADS, A_WINDOW = 8, 128
B_WIDTH, CONV_W = 512, 3
D_HEADS = 8
D_BRANCHES = ((128, 1), (512, 4), (2048, 16))
D_WINDOW = 2048
POOL_WINDOWS = (2, 4, 8, 16)
POOL_HIST = 15
ALPHA = float(4 ** 0.25)
EPS = 1e-5
QSCALE = HD ** -0.5
NEG = -1.0e30
N_HB = 8

GROUP = ((0, 384), (384, 384), (768, 320))
TILE_COLS = P
N_TILES = 9

EVEN_IN, EVEN_OUT, MLP_TILES, ODD_IN, ODD_OUT = 18, 8, 64, 16, 8
T_EIN = 0
T_EOUT = T_EIN + EVEN_IN
T_MLP = (T_EOUT + EVEN_OUT, T_EOUT + EVEN_OUT + MLP_TILES + ODD_IN + ODD_OUT)
T_OIN = T_MLP[0] + MLP_TILES
T_OOUT = T_OIN + ODD_IN
W_TILES = T_MLP[1] + MLP_TILES
NSLOT = 4
NRAW = 2

C_EBIN = 0
C_CONV = C_EBIN + EVEN_IN
C_EBOUT = C_CONV + CONV_W * 4
C_OBIN = C_EBOUT + KC
C_CSCALE = C_OBIN + ODD_IN
C_OBOUT = C_CSCALE + 4
C_LNG = C_OBOUT + KC
C_LNB = C_LNG + 4 * KC
N_COLS = C_LNB + 4 * KC

U_EIN = 0
U_EOUT = U_EIN + 3 * EVEN_IN
U_MLP = (U_EOUT + 3 * EVEN_OUT, U_EOUT + 3 * EVEN_OUT + N_HB * 24 + 3 * ODD_IN + 12 + 3 * ODD_OUT)
U_OIN = U_MLP[0] + N_HB * 24
U_OOUT = U_OIN + 3 * ODD_IN + 12
H_UNITS = 12 * N_HB

BACK_CHUNKS = ((0, 1, 2), (3, 4, 5), (6, 7))

XS_IN, XS_MIX0, XS_LN0, XS_LN1, XS_MIX1, XS_LN2 = 0, 3, 6, 30, 54, 57
XS_LN = (XS_LN0, XS_LN1, XS_LN2)

NB_D = 10
KEYS_D = NB_D * P + NS
COPY_PARTS = 12
JOBS_D = 8 * D_HEADS
PER_SEQ = JOBS_D // DEC_BATCH
QB_ORDER = (7, 0, 6, 1, 5, 2, 4, 3)
N_JOBS_A = 17


def build(nc, io):
    F32, F32R = mybir.dt.float32, mybir.dt.float32r
    ALU, ACT, AX = mybir.AluOpType, mybir.ActivationFunctionType, mybir.AxisListType
    ctx = ExitStack()
    with ctx:
        place = [nc.sbuf_base + (-nc.sbuf_base) % 64]

        def at(name, shape, dtype, offset):
            return nc.alloc_sbuf_tensor_at(name, shape, dtype, offset=offset)

        def room(nbytes):
            o = place[0]
            place[0] += -(-nbytes // 64) * 64
            return o

        def small(name, shape):
            n = 4
            for s in shape[1:]:
                n *= s
            return at(name, shape, F32, room(n))

        R = KC * NT * 4
        o_xr, o_hr, o_xs = room(R), room(R), room(2 * R)
        o_ws, o_wr, o_scr = room(NSLOT * 8192), room(NRAW * 4096), room(18432)

        X = at("X", [P, KC, NT], F32, o_xr)
        XS = at("XS", [P, 2, KC, NT], F32R, o_xs)
        HID = at("HID", [P, 2, 4, NT], F32R, o_hr)
        Y = at("Y", [P, KC, NT], F32, o_hr)
        WS = at("WS", [P, NSLOT, 2, 1024], F32R, o_ws)
        WR = at("WR", [P, NRAW, 1024], F32, o_wr)
        ZN = at("ZN", [P, 3, 1024], F32, o_scr)
        ZE = at("ZE", [P, 3, 1024], F32, o_hr)
        RT = at("RT", [P, 2, 384], F32, o_scr + 12288)
        ST = at("ST", [P, 2, 384], F32, o_scr + 15360)
        q = o_xr
        KTA = at("KTA", [P, NT], F32, q)
        VA = at("VA", [P, N_TILES, P], F32, q + 4352)
        CB = at("CB", [P, 2 + SEQ], F32, q + 8960)
        CV = at("CV", [P, NT], F32, q + 8960 + 4160)
        HT = at("HT", [P, NT], F32, q + 8960 + 4160 + 4352)
        KCT = at("KCT", [P, DEC_BATCH, P], F32, q + 21824)
        VCA = at("VCA", [P, DEC_BATCH, P], F32, q + 25920)
        KCA = at("KCA", [P, DEC_BATCH, P], F32, o_hr + R // 2)
        BAS = at("BAS", [P, 4, 192], F32, q + 30016)
        QS = at("QS", [P, DEC_BATCH, 4, DEC_SEQ], F32, q + 33088)
        SMA = at("SMA", [P, 4, 256], F32, o_scr)
        PTA = at("PTA", [P, 8, P], F32, o_scr + 4096)
        OTA = at("OTA", [P, 4, P], F32, o_scr + 8192)
        BA = at("BA", [P, 2, 4, 256], F32, o_scr + 10240)
        VT0 = at("VT0", [P, 2, 384], F32, o_scr)
        KTD = at("KTD", [P, 4, NT], F32, o_xr)
        VD = at("VD", [P, 8, 512], F32, o_xr + R // 2)
        PA = at("PA", [P, 16 + SEQ], F32, o_scr)
        PB = at("PB", [P, 16 + SEQ], F32, o_scr + 4160)
        PO = at("PO", [P, NT], F32, o_scr + 8320)
        SA = at("SA", [P, DEC_BATCH, 23], F32, o_scr + 12672)
        SB = at("SB", [P, DEC_BATCH, 23], F32, o_scr + 13408)
        VT1 = at("VT1", [P, 2, 384], F32, o_scr + 14144)
        TH = at("TH", [P, 2, SEQ], F32, o_xs)
        SMD = at("SMD", [P, 3, SEQ], F32, o_xs + 8192)
        PTD = at("PTD", [P, 2, 8, P], F32, o_xs + 20480)
        KCD = at("KCD", [P, NB_D, 512], F32, o_xs + 28672)
        VCD = at("VCD", [P, NB_D, 512], F32, o_xs + 49152)
        KTC = at("KTC", [P, 4, 512], F32, o_wr)
        SMS = at("SMS", [P, KEYS_D], F32, o_scr)
        PTS = at("PTS", [P, NB_D + 1, P], F32, o_scr + 5376)
        BS = at("BS", [P, KEYS_D], F32, o_scr + 11008)
        BNEW = at("BNEW", [P, DEC_BATCH, NS], F32, o_scr + 16384)
        QBD = at("QBD", [P, 2, 4, 32], F32, o_xr + 33792)
        IDN = small("IDN", [P, P])
        COLS = small("COLS", [P, N_COLS])
        SINK = small("SINK", [P, 12])
        RC = small("RC", [P, 4, 16])
        CS = small("CS", [P, 4, DEC_BATCH, 2 + DEC_SEQ])
        BCO = small("BCO", [P, 4, 2])
        KN = small("KN", [NS, 512])
        VN = small("VN", [NS, 512])
        US = small("US", [P, 4, DEC_BATCH, POOL_HIST + DEC_SEQ])
        UO = small("UO", [P, 4, POOL_HIST])
        BNS = small("BNS", [P, 12])
        MV = small("MV", [P, 2])
        VE = small("VE", [P, 1])
        SD = small("SD", [P, 1])
        RS = small("RS", [P, 1])
        NW = small("NW", [P, 1])
        MX = small("MX", [P, 2, 4])
        MXS = small("MXS", [P, 3])
        NM = small("NM", [P, 2, 4])
        DS = small("DS", [P, 4])
        ES = small("ES", [P, 4])
        SUM = small("SUM", [P, 2, 4])
        RD = small("RD", [P, 2, 4])
        o_gw = room(2048)
        GW = at("GW", [P, 4, P], F32, o_gw)
        QP = at("QP", [P, 2, 2, P], F32, o_gw)
        OS = small("OS", [P, P])
        assert place[0] <= nc.sbuf_top, (place[0], nc.sbuf_top)

        PS = ctx.enter_context(nc.psum_tensor("PS", [P, 8, 512], F32))

        def bank(b, n=512):
            return PS[:, b, 0:n]

        def sem(name):
            return ctx.enter_context(nc.semaphore(name))

        x_in = [sem(f"x_in{g}") for g in range(3)]
        xr_in = [[sem(f"xr{l}_in{g}") for g in range(3)] for l in range(2)]
        spilled = sem("spilled")
        ident_in, cols_in, kca_in, biasa_in = sem("ident_in"), sem("cols_in"), sem("kca_in"), sem("biasa_in")
        states_in, qs_ready, bas_in, vca_in = sem("states_in"), sem("qs_ready"), sem("bas_in"), sem("vca_in")
        w_in = [sem(f"w_in{r}") for r in range(NRAW)]
        w_hi, w_split = sem("w_hi"), sem("w_split")
        p_mm, p_evac = sem("p_mm"), sem("p_evac")
        h_mm, h_evac, h_sq, hid_hi, hid_ready = sem("h_mm"), sem("h_evac"), sem("h_sq"), sem("hid_hi"), sem("hid_ready")
        x_hi, x_split, x_scaled = sem("x_hi"), sem("x_split"), sem("x_scaled")
        ft_mm, ve_ready, std_ready, zn_ready = sem("ft_mm"), sem("ve_ready"), sem("std_ready"), sem("zn_ready")
        bt_mm, b_evac, b_hi, b_evac_odd = sem("bt_mm"), sem("b_evac"), sem("b_hi"), sem("b_evac_odd")
        dve_link, vt_mm, vt_evac = sem("dve_link"), sem("vt_mm"), sem("vt_evac")
        kn_mm, kn_evac = sem("kn_mm"), sem("kn_evac")
        kct_mm, kct_evac = sem("kct_mm"), sem("kct_evac")
        sa_mm, sa_max, sa_exp, sa_prob, pta_mm, pta_evac = (sem("sa_mm"), sem("sa_max"), sem("sa_exp"),
                                                            sem("sa_prob"), sem("pta_mm"), sem("pta_evac"))
        oa_mm, oa_evac, ota_mm, ota_evac = sem("oa_mm"), sem("oa_evac"), sem("ota_mm"), sem("ota_evac")
        th_in = [sem("th_in0"), sem("th_in1")]
        sd_mm, sd_max, sd_exp, ptd_mm, ptd_evac = sem("sd_mm"), sem("sd_max"), sem("sd_exp"), sem("ptd_mm"), sem("ptd_evac")
        od_mm, od_evac = sem("od_mm"), sem("od_evac")
        ks_in, vs_in, bs_in = [sem(f"ks_in{e}") for e in range(3)], sem("vs_in"), sem("bs_in")
        ktc_mm, ktc_evac, qbd_ready, ss_mm, ss_max, ss_exp = (
            sem("ktc_mm"), sem("ktc_evac"), sem("qbd_ready"), sem("ss_mm"), sem("ss_max"), sem("ss_exp"))
        pts_mm, pts_evac, os_mm, os_evac = sem("pts_mm"), sem("pts_evac"), sem("os_mm"), sem("os_evac")
        bco_ready, uo_ready, qbd_zero, po_ready = sem("bco_ready"), sem("uo_ready"), sem("qbd_zero"), sem("po_ready")
        ss_taken = sem("ss_taken")
        qp_zero, qp_ready, sd_prob = sem("qp_zero"), sem("qp_ready"), sem("sd_prob")
        os_scaled, ost_mm = sem("os_scaled"), sem("ost_mm")
        copied, stored_a, stored_d, stored_y = sem("copied"), sem("stored_a"), sem("stored_d"), sem("stored_y")

        def back_bank(l, g, k):
            return (2, 3, 6, 7)[k % 4] if (l, g) == (3, 2) else 2 + k % 2

        def rows_out(l, g):
            return ZE if (l, g) == (3, 2) else ZN

        def rows_in(l, t):
            b = 0 if t % 2 else 6 if t >= 6 and l % 2 == 0 else 4
            return PS[:, b:b + 2, :].rearrange("p a b -> p (a b)")

        def col(i, n=P):
            return COLS[0:n, i:i + 1]

        def tile_rows(t):
            return NS if t == N_TILES - 1 else P

        def job_a(n):
            qb, half = divmod(n, 2)
            if n == N_JOBS_A - 1:
                return 192, 2, 0
            return (P, 1, 0) if qb == 0 else (2 * P, 2, (qb - 1) * P)

        def job_d(m):
            return m // PER_SEQ, QB_ORDER[m % PER_SEQ]

        def pieces_d(m):
            nk = job_d(m)[1] + 1
            return [(k, min(4, nk - k)) for k in range(0, nk, 4)]

        piece_base = [0]
        for m in range(64):
            piece_base.append(piece_base[-1] + len(pieces_d(m)))

        def scores_bank(m):
            return 2 * (m % 2)

        def keys_bank(n):
            return 3 + 4 * (n % 2)

        PT_BANK_S = (3, 7, 6)
        PIECES_S = (4, 4, 2)

        block = ctx.enter_context(nc.Block())

        @block.sync
        def _(sp):
            def weight(t, first=0):
                if t >= NRAW:
                    sp.wait_ge(w_split, t - NRAW + 1)
                sp.dma_start(WR[:, t % NRAW, :], io["w"][t, :, :]).then_inc(w_in[t % NRAW], 16)

            def weight_loop(i, t0, j):
                t = 8 * i + (t0 + j)
                sp.wait_ge(w_split, t - NRAW + 1)
                sp.dma_start(WR[:, (t0 + j) % NRAW, :],
                             io["w"][bass.ds(t, 1), :, :].rearrange("a p n -> (a p) n")).then_inc(w_in[(t0 + j) % NRAW], 16)

            for g, (c0, gw) in enumerate(GROUP):
                sp.dma_start(X[:, :, c0:c0 + gw], io["x"][:, :, c0:c0 + gw]).then_inc(x_in[g], 16)
                for t in ((0, 1), (2,), (3,))[g]:
                    weight(t)
            for t in range(4, T_EOUT + 6):
                weight(t)
            sp.wait_ge(ota_evac, 10)
            sp.wait_ge(p_evac, U_EOUT)
            sp.wait_ge(kn_evac, 1)
            sp.wait_ge(bco_ready, 4)
            sp.dma_start(io["a_k"][:, :], KTA[:, SEQ - A_WINDOW:SEQ]).then_inc(stored_a, 16)
            sp.dma_start(io["a_v"][:, :], VA[:, 7, :]).then_inc(stored_a, 16)
            for b in range(DEC_BATCH):
                rows = slice(b * DEC_SEQ, (b + 1) * DEC_SEQ)
                sp.dma_start(io["a_ks"][b, A_WINDOW - DEC_SEQ:, :], KN[rows, 0:P]).then_inc(stored_a, 16)
                sp.dma_start(io["a_vs"][b, A_WINDOW - DEC_SEQ:, :], VA[rows, 8, :]).then_inc(stored_a, 16)
            sp.dma_start(io["b_c"][:, :, :], BCO[:, :, :]).then_inc(stored_a, 16)
            for j in range(4):
                sp.dma_start(io["b_cs"][:, j, :, :], CS[:, j, :, DEC_SEQ:]).then_inc(stored_a, 16)
            sp.wait_ge(stored_a, 16 * 23)
            for g, (c0, gw) in enumerate(GROUP):
                sp.dma_start(X[:, :, c0:c0 + gw], io["x"][:, :, c0:c0 + gw]).then_inc(xr_in[0][g], 16)
            for t in range(T_EOUT + 6, T_MLP[0] + 4):
                weight(t)
            with sp.Fori(0, N_HB - 1) as i:
                for j in range(8):
                    weight_loop(i, T_MLP[0] + 4, j)
            for t in range(T_OIN - 4, T_OIN + 6):
                weight(t)
            for g, (c0, gw) in enumerate(GROUP):
                sp.wait_ge(x_scaled, 24 + 8 * (g + 1))
                sp.dma_start(io["spill"][:, :, c0:c0 + gw], X[:, :, c0:c0 + gw]).then_inc(spilled, 16)
            for t in range(T_OIN + 6, T_OIN + ODD_IN):
                weight(t)
            for t in range(T_OOUT, T_OOUT + 2):
                weight(t)
            sp.wait_ge(p_mm, U_OOUT - 3)
            for h in range(2):
                sp.dma_start(TH[:, h, :], io["th"][h, :, :]).then_inc(th_in[h], 16)
            for t in range(T_OOUT + 2, T_OOUT + 4):
                weight(t)

            def load_cache(dst, name, b, e, done):
                far = io[name][b, :, :].rearrange("(a s) f -> a s f", s=16)
                if e < 2:
                    sp.dma_start(dst[:, 4 * e:4 * e + 4, :], far[:, 4 * e:4 * e + 4, :]).then_inc(done, 16)
                else:
                    for r in range(4):
                        sp.dma_start(dst[32 * r:32 * r + 32, 8:10, :], far[96:128, 8 + 2 * r:10 + 2 * r, :])\
                          .then_inc(done, 16)

            for e in range(3):
                load_cache(KCD, "cache_d_k", 0, e, ks_in[e])
            sp.wait_ge(p_evac, U_OOUT)
            sp.wait_ge(vt_mm, 15)
            sp.dma_start(BS[:, 0:NB_D * P], io["bs"][:, :]).then_inc(bs_in, 16)
            sp.dma_start(BNEW[:, :, :], io["bnew"][:, :, :]).then_inc(bs_in, 16)
            for e in range(3):
                load_cache(VCD, "cache_d_v", 0, e, vs_in)
            sp.wait_ge(kn_evac, 2)
            sp.wait_ge(vt_evac, 15)
            sp.wait_ge(uo_ready, 4)
            for c in range(4):
                sp.dma_start(io["d_k"][:, c, :], KTD[:, c, 0:SEQ]).then_inc(stored_d, 16)
            sp.dma_start(io["d_v"].rearrange("(t p) f -> p t f", p=P), VD[:, :, :]).then_inc(stored_d, 16)
            for b in range(DEC_BATCH):
                rows = slice(b * DEC_SEQ, (b + 1) * DEC_SEQ)
                sp.dma_start(io["d_ks"][b, D_WINDOW - DEC_SEQ:, :], KN[rows, :]).then_inc(stored_d, 16)
                sp.dma_start(io["d_vs"][b, D_WINDOW - DEC_SEQ:, :], VN[rows, :]).then_inc(stored_d, 16)
            sp.dma_start(io["c_p"][:, :, :], UO[:, :, :]).then_inc(stored_d, 16)
            for c in range(4):
                sp.dma_start(io["c_ps"][:, c, :, :], US[:, c, :, DEC_SEQ:]).then_inc(stored_d, 16)
            for b in range(1, DEC_BATCH):
                for e in range(2):
                    sp.wait_ge(ktc_mm, 12 * (b - 1) + 4 * (e + 1))
                    load_cache(KCD, "cache_d_k", b, e, ks_in[e])
                if b >= 2:
                    sp.wait_ge(os_mm, b - 1)
                    for e in range(3):
                        load_cache(VCD, "cache_d_v", b - 1, e, vs_in)
                sp.wait_ge(ktc_mm, 12 * b)
                load_cache(KCD, "cache_d_k", b, 2, ks_in[2])
                h = b + 1
                if h < D_HEADS:
                    sp.wait_ge(sd_max, 8 * (h - 1))
                    sp.dma_start(TH[:, h % 2, :], io["th"][h, :, :]).then_inc(th_in[h % 2], 16)
            sp.wait_ge(os_mm, DEC_BATCH - 1)
            for e in range(3):
                load_cache(VCD, "cache_d_v", DEC_BATCH - 1, e, vs_in)
            sp.wait_ge(stored_d, 16 * 26)
            sp.wait_ge(os_evac, DEC_BATCH)
            sp.wait_ge(spilled, 48)
            for t in range(T_OOUT + 4, T_OOUT + 6):
                weight(t)
            for g, (c0, gw) in enumerate(GROUP):
                sp.dma_start(X[:, :, c0:c0 + gw], io["spill"][:, :, c0:c0 + gw]).then_inc(xr_in[1][g], 16)
            for t in range(T_OOUT + 6, T_MLP[1] + 4):
                weight(t)
            with sp.Fori(0, N_HB - 1) as i:
                for j in range(8):
                    weight_loop(i, T_MLP[1] + 4, j)
            for t in range(W_TILES - 4, W_TILES):
                weight(t)
            for g, (c0, gw) in enumerate(GROUP):
                sp.wait_ge(b_evac, 72 + 8 * (g + 1) - (4 if g == 2 else 0))
                if g == 2:
                    sp.wait_ge(b_evac_odd, 4)
                sp.dma_start(io["y"][:, :, c0:c0 + gw], X[:, :, c0:c0 + gw]).then_inc(stored_y, 16)
            sp.wait_ge(stored_y, 48)
            sp.wait_ge(copied, 16 * (2 + 2 * N_HB * COPY_PARTS))

        @block.gpsimd
        def _(pool):
            def rest(slot, raw, hi):
                pool.wait_ge(w_hi, hi)
                pool.tensor_tensor(WS[:, slot, 1, :], WR[:, raw, :], WS[:, slot, 0, :].bitcast(F32),
                                   ALU.subtract).then_inc(w_split, 1)

            def one(t):
                rest(t % NSLOT, t % NRAW, t + 1)

            def ln_low(l, phase, quarter):
                if quarter < 3:
                    g = phase - 2
                    c0, gw = GROUP[g]
                    for k in BACK_CHUNKS[quarter]:
                        pool.wait_ge(b_hi, 24 * l + 8 * g + k + 1)
                        pool.tensor_tensor(XS[:, 1, k, c0:c0 + gw], X[:, k, c0:c0 + gw],
                                           XS[:, 0, k, c0:c0 + gw].bitcast(F32), ALU.subtract).then_inc(x_split, 1)

            def between(l, t0):
                for j in range(4):
                    one(t0 + j)
                    ln_low(l, 2, j)
                for phase in (3, 4):
                    for j in range(4):
                        ln_low(l, phase, j)

            def mlp(l):
                t0 = T_MLP[l]
                between(2 * l, t0)
                with pool.Fori(0, N_HB - 1) as i:
                    for j in range(8):
                        t = t0 + 4 + j
                        rest(t % NSLOT, t % NRAW, 8 * i + (t + 1))
                for j in range(4):
                    one(t0 + 60 + j)

            def q_pad(m):
                h, qb = job_d(m)
                lo = (h % 2) * HD
                if m >= 2:
                    pool.wait_ge(sd_mm, m - 1)
                pool.tensor_copy(QP[lo:lo + HD, h % 2, m % 2, :], Y[lo:lo + HD, 4 + h // 2, qb * P:qb * P + P])\
                    .then_inc(qp_ready, 1)

            for t in range(T_MLP[0]):
                one(t)
            mlp(0)
            between(1, T_OIN)
            for t in range(T_OIN + 4, T_OOUT + 4):
                one(t)
            pool.wait_ge(p_mm, U_OOUT)
            pool.memset(QP[:, :, :, :], 0.0).then_inc(qp_zero, 1)
            pool.wait_ge(qp_zero, 1)
            for m in range(JOBS_D):
                q_pad(m)
            for t in range(T_OOUT + 4, T_MLP[1]):
                one(t)
            mlp(1)

        @block.scalar
        def _(act):
            act.dma_start(IDN[:, :], io["ident"][:, :]).then_inc(ident_in, 16)
            act.dma_start(COLS[:, :], io["cols"][:, :]).then_inc(cols_in, 16)
            act.dma_start(SINK[:, :], io["sink"][:, :]).then_inc(cols_in, 16)
            act.dma_start(RC[:, :, :], io["rc"][:, :, :]).then_inc(cols_in, 16)
            act.dma_start(GW[:, :, :], io["gw"][:, :, :]).then_inc(cols_in, 16)

            def split_high(stage, src):
                for g, (c0, gw) in enumerate(GROUP):
                    if stage == 0:
                        act.wait_ge(x_in[g], 16)
                    for k in (0, KC // 2):
                        act.activation(XS[:, 0, k:k + KC // 2, c0:c0 + gw], src[:, k:k + KC // 2, c0:c0 + gw],
                                       ACT.Copy).then_inc(x_hi, 1)

            split_high(0, X)
            act.dma_start(KCA[:, :, :], io["cache_a_k"].rearrange("b p f -> p b f")).then_inc(kca_in, 16)
            for j in range(4):
                act.dma_start(CS[:, j, :, 0:2], io["b_state"][:, j, :, :]).then_inc(states_in, 16)
                act.dma_start(US[:, j, :, 0:POOL_HIST], io["c_state"][:, j, :, :]).then_inc(states_in, 16)
            act.dma_start(BA[:, :, :, :], io["ba"][:, :, :, :]).then_inc(biasa_in, 16)
            act.dma_start(io["a_ks"][:, 0:A_WINDOW - DEC_SEQ, :], io["cache_a_k"][:, DEC_SEQ:, :]).then_inc(copied, 16)
            act.dma_start(io["a_vs"][:, 0:A_WINDOW - DEC_SEQ, :], io["cache_a_v"][:, DEC_SEQ:, :]).then_inc(copied, 16)

            def ln_weave(l, phase, quarter, parts="BF"):
                if "B" in parts and 0 <= phase - 2 <= 2 and quarter < 3:
                    g = phase - 2
                    c0, gw = GROUP[g]
                    for k in BACK_CHUNKS[quarter]:
                        n = 24 * l + 8 * g + k
                        if (l, g) == (3, 2) and k % 2:
                            continue
                        act.wait_ge(bt_mm, n + 1)
                        act.activation(X[:, k, c0:c0 + gw], bank(back_bank(l, g, k), gw), ACT.Identity,
                                       scale=col(C_LNG + KC * l + k), bias=col(C_LNB + KC * l + k)).then_inc(b_evac, 1)
                        if l < 3:
                            act.wait_ge(b_evac, n + 1)
                            act.activation(XS[:, 0, k, c0:c0 + gw], X[:, k, c0:c0 + gw], ACT.Copy).then_inc(b_hi, 1)
                if "F" in parts and 0 <= phase - 1 <= 2 and quarter > 0:
                    n = 9 * l + 3 * (phase - 1) + quarter - 1
                    rows = tile_rows(3 * (phase - 1) + quarter - 1)
                    act.wait_ge(ve_ready, n + 1)
                    act.activation(SD[0:rows, :], VE[0:rows, :], ACT.Sqrt).then_inc(std_ready, 1)

            def v_evac(n, g, dst, last):
                act.wait_ge(vt_mm, n + 1)
                b = PS[:, 4 + n % 2, 0:384].rearrange("p (t f) -> p t f", t=3)
                if g < 2:
                    act.activation(dst, b, ACT.Copy).then_inc(vt_evac, 1)
                else:
                    act.activation(dst, b[:, 0:2, :], ACT.Copy)
                    act.activation(last, b[0:NS, 2, :], ACT.Copy).then_inc(vt_evac, 1)

            for g in range(3):
                nt = 3 if g < 2 else 2
                v_evac(g, g, VA[:, 3 * g:3 * g + nt, :], VA[0:NS, 8, :])
            act.wait_ge(kn_mm, 1)
            act.activation(KN[:, 0:P], PS[0:NS, 4, 0:P], ACT.Copy).then_inc(kn_evac, 1)
            act.wait_ge(x_split, 3)
            act.dma_start(VCA[:, :, :], io["cache_a_v"].rearrange("b p f -> p b f")).then_inc(vca_in, 16)
            act.dma_start(BAS[:, :, :], io["bas"][:, :, :]).then_inc(bas_in, 16)
            for h in range(2):
                act.wait_ge(kct_mm, h + 1)
                act.activation(KCT[:, 4 * h:4 * h + 4, :],
                               PS[:, 2 + h, :].rearrange("p (b f) -> p b f", b=4), ACT.Copy).then_inc(kct_evac, 1)

            def a_exp(n):
                w, nk, k0 = job_a(n)
                act.wait_ge(sa_max, n + 1)
                act.activation(ES[:, :], DS[:, :], ACT.Exp)
                for c in range(4):
                    ins = act.activation(SMA[:, c, 0:w], SMA[:, c, 0:w], ACT.Exp, bias=NM[:, 0, c:c + 1],
                                         accum_out=SUM[:, 0, c:c + 1])
                ins.then_inc(sa_exp, 1)

            def a_pt(n):
                w, nk, k0 = job_a(n)
                act.wait_ge(pta_mm, n + 1)
                src = PS[:, 2:4, :].rearrange("p a (b f) -> p (a b) f", f=P)
                if n < N_JOBS_A - 1:
                    act.activation(PTA[:, 0:4 * nk, :], src[:, 0:4 * nk, :], ACT.Copy).then_inc(pta_evac, 1)
                else:
                    act.activation(PTA[:, 0:4, :], src[:, 0:4, :], ACT.Copy)
                    act.activation(PTA[0:NS, 4:8, :], src[0:NS, 4:8, :], ACT.Copy).then_inc(pta_evac, 1)

            def a_out(qb):
                act.wait_ge(ota_mm, qb + 1)
                act.activation(Y[:, 0:4, qb * P:qb * P + P], PS[:, 5, :].rearrange("p (c f) -> p c f", c=4),
                               ACT.Copy).then_inc(ota_evac, 1)

            for n in range(N_JOBS_A):
                a_exp(n)
                a_pt(n)
                if n >= 2 and n % 2 == 0:
                    a_out(n // 2 - 1)
            for quad in range(2):
                act.wait_ge(ota_mm, 9)
                for bb in range(4):
                    b = 4 * quad + bb
                    ins = act.activation(Y[:, 0:4, SEQ + 8 * b:SEQ + 8 * b + 8],
                                         PS[:, 5, P * quad + 32 * bb:P * quad + 32 * bb + 32].rearrange("p (c i) -> p c i", c=4),
                                         ACT.Copy)
                ins.then_inc(ota_evac, 1)
            act.wait_ge(ota_evac, 10)
            act.wait_ge(p_evac, U_EOUT)
            split_high(1, Y)

            def hidden_super(l, i, weave, copy):
                for g, (c0, gw) in enumerate(GROUP):
                    for j in range(4):
                        u = 4 * g + j
                        n = 12 * i + (H_UNITS * l + u)
                        act.wait_ge(h_mm, n + 1)
                        act.activation(RT[:, u % 2, 0:gw], bank(4 + u % 2, gw), ACT.Relu).then_inc(h_evac, 1)
                        act.wait_ge(h_evac, n + 1)
                        if not (isinstance(n, int) and n < 2):
                            act.wait_ge(hid_ready, n - 1)
                        act.activation(ST[:, u % 2, 0:gw], RT[:, u % 2, 0:gw], ACT.Square).then_inc(h_sq, 1)
                        act.wait_ge(h_sq, n + 1)
                        act.activation(HID[:, 0, j, c0:c0 + gw], ST[:, u % 2, 0:gw], ACT.Copy).then_inc(hid_hi, 1)
                        cache_copy(*copy, u)
                        if weave is not None and g < 2:
                            ln_weave(weave, 3 + g, j)

            def cache_copy(name, out, b, part):
                n = (D_WINDOW - DEC_SEQ) // COPY_PARTS
                if isinstance(b, int):
                    src, dst = io[name][b:b + 1], io[out][b:b + 1]
                else:
                    src, dst = io[name][bass.ds(b, 1)], io[out][bass.ds(b, 1)]
                src = src[:, DEC_SEQ + n * part:DEC_SEQ + n * (part + 1), :].rearrange("a s f -> a (s f)")
                dst = dst[:, n * part:n * (part + 1), :].rearrange("a s f -> a (s f)")
                act.dma_start(dst.rearrange("a (k f) -> (a k) f", k=16),
                              src.rearrange("a (k f) -> (a k) f", k=16)).then_inc(copied, 16)

            def mlp(l, name, out):
                for g in range(3):
                    for j in range(4):
                        ln_weave(2 * l, g, j)
                hidden_super(l, 0, 2 * l, (name, out, N_HB - 1))
                with act.Fori(0, N_HB - 1) as i:
                    hidden_super(l, i + 1, None, (name, out, i))
                for g in range(3):
                    for j in range(4):
                        ln_weave(2 * l + 1, g, j)

            mlp(0, "cache_d_k", "d_ks")
            for g in range(2):
                for j in range(4):
                    ln_weave(1, 3 + g, j)
            for g in range(3):
                nt = 3 if g < 2 else 2
                for j in range(4):
                    v_evac(3 + 4 * g + j, g, VD[:, 3 * g:3 * g + nt, j * P:j * P + P], VN[0:NS, j * P:j * P + P])
            act.wait_ge(kn_mm, 2)
            act.activation(KN[:, :], PS[0:NS, 3, :], ACT.Copy).then_inc(kn_evac, 1)

            def d_exp(m):
                w = P * (job_d(m)[1] + 1)
                act.wait_ge(sd_max, m + 1)
                act.activation(SMD[:, m % 3, 0:w], SMD[:, m % 3, 0:w], ACT.Exp, bias=NM[:, m % 2, 0:1],
                               accum_out=SUM[:, m % 2, 0:1]).then_inc(sd_exp, 1)

            def q_block_diag(b):
                s = b % 2
                act.activation(QBD[0:HD, s, :, 0:DEC_SEQ], Y[0:HD, 4:8, SEQ + 8 * b:SEQ + 8 * b + 8], ACT.Copy)
                act.activation(QBD[HD:P, s, :, DEC_SEQ:2 * DEC_SEQ], Y[HD:P, 4:8, SEQ + 8 * b:SEQ + 8 * b + 8],
                               ACT.Copy).then_inc(qbd_ready, 1)

            def s_pt(b, e):
                nb = PIECES_S[e]
                act.wait_ge(pts_mm, 3 * b + e + 1)
                pb = PS[:, PT_BANK_S[e], :].rearrange("p (b f) -> p b f", f=P)
                ins = act.activation(PTS[:, 4 * e:4 * e + nb, :], pb[:, 0:nb, :], ACT.Copy)
                if e == 2:
                    ins = act.activation(PTS[0:NS, NB_D, :], pb[0:NS, 2, :], ACT.Copy)
                ins.then_inc(pts_evac, 1)

            act.wait_ge(qbd_zero, 1)
            q_block_diag(0)
            d_exp(0)
            for m in range(JOBS_D):
                b, step = divmod(m, PER_SEQ)
                for e, (k, nk) in enumerate(pieces_d(m)):
                    n = piece_base[m] + e
                    act.wait_ge(ptd_mm, n + 1)
                    act.activation(PTD[:, m % 2, k:k + nk, :], PS[:, 4, 0:nk * P].rearrange("p (b f) -> p b f", f=P),
                                   ACT.Copy).then_inc(ptd_evac, 1)
                    if e == 0 and m + 1 < JOBS_D:
                        d_exp(m + 1)
                if step == 0 and b:
                    s_pt(b - 1, 2)
                if step == 7:
                    s_pt(b, 0)
                    s_pt(b, 1)
                if step == 5 and b + 1 < DEC_BATCH:
                    q_block_diag(b + 1)
                if step == 6:
                    act.wait_ge(ss_max, b + 1)
                    act.activation(SMS[:, :], SMS[:, :], ACT.Exp, bias=NM[:, 0, 1:2], accum_out=SUM[:, 0, 1:2])\
                       .then_inc(ss_exp, 1)
            s_pt(DEC_BATCH - 1, 2)
            act.wait_ge(od_evac, JOBS_D)
            act.wait_ge(os_evac, DEC_BATCH)
            split_high(2, Y)
            mlp(1, "cache_d_v", "d_vs")
            for j in range(3):
                ln_weave(3, 3, j, "B")
                ln_weave(3, 3, j + 1, "F")
            for j in range(3):
                ln_weave(3, 4, j, "B")

        @block.vector
        def _(dve):
            links = [0]


            def link(ins):
                links[0] += 1
                ins.then_inc(dve_link, 1)
                dve.wait_ge(dve_link, links[0])

            def split_low(stage, src, groups=(0, 1, 2)):
                for g in groups:
                    c0, gw = GROUP[g]
                    for h in range(2):
                        k = slice(h * KC // 2, (h + 1) * KC // 2)
                        dve.wait_ge(x_hi, 6 * stage + 2 * g + h + 1)
                        ins = dve.tensor_tensor(XS[:, 1, k, c0:c0 + gw], src[:, k, c0:c0 + gw],
                                                XS[:, 0, k, c0:c0 + gw].bitcast(F32), ALU.subtract)
                    ins.then_inc(x_split, 1)

            def w_high(t):
                dve.wait_ge(w_in[t % NRAW], 16 * (t // NRAW + 1))
                dve.tensor_copy(WS[:, t % NSLOT, 0, :], WR[:, t % NRAW, :]).then_inc(w_hi, 1)

            def w_high_loop(i, t):
                dve.wait_ge(w_in[t % NRAW], 64 * i + 16 * (t // NRAW + 1))
                dve.tensor_copy(WS[:, t % NSLOT, 0, :], WR[:, t % NRAW, :]).then_inc(w_hi, 1)

            def ln_weave(l, phase, quarter, parts="BF"):
                if "B" in parts and 0 <= phase - 2 <= 2 and quarter > 0 and l < 3:
                    g = phase - 2
                    c0, gw = GROUP[g]
                    for k in BACK_CHUNKS[quarter - 1]:
                        dve.wait_ge(x_split, XS_LN[l] + 8 * g + k + 1)
                        dve.tensor_scalar(X[:, k, c0:c0 + gw], X[:, k, c0:c0 + gw], ALPHA, None, ALU.mult)\
                           .then_inc(x_scaled, 1)
                if "F" in parts and 0 <= phase - 1 <= 2 and quarter > 0:
                    g, tt = phase - 1, quarter - 1
                    n = 9 * l + 3 * g + tt
                    r = tile_rows(3 * g + tt)
                    FT = rows_in(l, 3 * g + tt)
                    dve.wait_ge(ft_mm, n + 1)
                    dve.bn_stats(BNS[0:r, 0:6], FT[0:r, 0:512])
                    link(dve.bn_stats(BNS[0:r, 6:12], FT[0:r, 512:1024]))
                    link(dve.bn_aggr(MV[0:r, :], BNS[0:r, :]))
                    dve.tensor_scalar(VE[0:r, :], MV[0:r, 1:2], EPS, None, ALU.add).then_inc(ve_ready, 1)
                    dve.wait_ge(std_ready, n + 1)
                    link(dve.reciprocal(RS[0:r, :], SD[0:r, :]))
                    link(dve.scalar_tensor_tensor(out=NW[0:r, :], in0=RS[0:r, :], scalar=VE[0:r, :], in1=RS[0:r, :],
                                                  op0=ALU.mult, op1=ALU.mult))
                    link(dve.tensor_scalar(NW[0:r, :], NW[0:r, :], -0.5, 1.5, ALU.mult, ALU.add))
                    link(dve.tensor_tensor(RS[0:r, :], RS[0:r, :], NW[0:r, :], ALU.mult))
                    if n >= 3:
                        dve.wait_ge(bt_mm, 24 * l + 8 * g - (8 if (l, g) == (3, 2) else 0))
                    dve.tensor_scalar(rows_out(l, g)[0:r, tt, :], FT[0:r, :], MV[0:r, 0:1], RS[0:r, 0:1],
                                      ALU.subtract, ALU.mult).then_inc(zn_ready, 1)

            def taken(u):
                return bank(6 + u % 2)

            w_high(0)
            w_high(1)
            split_low(0, X, (0,))
            w_high(2)
            dve.wait_ge(cols_in, 64)

            def ein_evac(t, g, u):
                c0, gw = GROUP[g]
                ps = taken(u)[:, 0:gw]
                bias = col(C_EBIN + t)
                pw = gw - (NS if g == 2 else 0)
                dve.wait_ge(p_mm, u + 1)
                if t == 0:
                    dve.wait_ge(x_split, g + 1)
                    dve.tensor_scalar(KTA[:, c0:c0 + gw], ps, bias, None, ALU.add).then_inc(p_evac, 1)
                elif t == 1:
                    if g >= 2:
                        dve.wait_ge(vt_mm, g - 1)
                    dve.tensor_scalar(VT0[:, g % 2, 0:gw], ps, bias, None, ALU.add).then_inc(p_evac, 1)
                elif t < 6:
                    dve.tensor_scalar(Y[:, t - 2, c0:c0 + gw], ps, bias, QSCALE, ALU.add, ALU.mult).then_inc(p_evac, 1)
                else:
                    j, kind = divmod(t - 6, 3)
                    if kind == 0:
                        dve.tensor_scalar(HT[:, c0:c0 + gw], ps, bias, None, ALU.add).then_inc(p_evac, 1)
                        dve.wait_ge(p_evac, u + 1)
                    elif kind == 1:
                        link(dve.scalar_tensor_tensor(out=CB[:, 2 + c0:2 + c0 + pw], in0=ps[:, 0:pw], scalar=bias,
                                                      in1=HT[:, c0:c0 + pw], op0=ALU.add, op1=ALU.mult))
                        parts = [(CV[:, c0:c0 + pw], [CB[:, c0 + i:c0 + i + pw] for i in range(CONV_W)])]
                        if g == 2:
                            link(dve.scalar_tensor_tensor(
                                out=CS[:, j, :, 2:], in0=ps[:, pw:gw].rearrange("p (b i) -> p b i", b=DEC_BATCH), scalar=bias,
                                in1=HT[:, SEQ:NT].rearrange("p (b i) -> p b i", b=DEC_BATCH), op0=ALU.add, op1=ALU.mult))
                            parts.append((CV[:, SEQ:NT].rearrange("p (b i) -> p b i", b=DEC_BATCH),
                                          [CS[:, j, :, i:i + DEC_SEQ] for i in range(CONV_W)]))
                            dve.tensor_copy(BCO[:, j, :], CB[:, SEQ:SEQ + 2]).then_inc(bco_ready, 1)
                        for out, taps in parts:
                            link(dve.tensor_scalar(out, taps[0], col(C_CONV + j), None, ALU.mult))
                            for i in (1, 2):
                                ins = dve.scalar_tensor_tensor(out=out, in0=taps[i], scalar=col(C_CONV + 4 * i + j),
                                                               in1=out, op0=ALU.mult, op1=ALU.add)
                                if i == 1 or out is not parts[-1][0]:
                                    link(ins)
                        ins.then_inc(p_evac, 1)
                        dve.wait_ge(p_evac, u + 1)
                    else:
                        dve.scalar_tensor_tensor(out=Y[:, 4 + j, c0:c0 + gw], in0=ps, scalar=bias,
                                                 in1=CV[:, c0:c0 + gw], op0=ALU.add, op1=ALU.mult).then_inc(p_evac, 1)

            def a_scores(n):
                w, nk, k0 = job_a(n)
                half = n % 2
                sample = n == N_JOBS_A - 1
                if n == 0:
                    dve.wait_ge(biasa_in, 16)
                    dve.wait_ge(vt_mm, 3)
                if sample:
                    dve.wait_ge(bas_in, 16)
                dve.wait_ge(sa_mm, n + 1)
                s = PS[:, 0:2, :].rearrange("p a (b f) -> p (a b) f", f=256)
                for c in range(4):
                    bias = BAS[:, c, :] if sample else BA[:, half, c, 256 - w:256]
                    sink = SINK[:, 8 + c:9 + c] if sample else SINK[:, 4 * half + c:4 * half + c + 1]
                    ins = dve.tensor_tensor_reduce(out=SMA[:, c, 0:w], in0=s[:, c, 0:w], in1=bias, scale=1.0,
                                                   scalar=sink, op0=ALU.add, op1=ALU.max,
                                                   accum_out=MX[:, 0, c:c + 1])
                link(ins)
                link(dve.tensor_scalar(NM[:, 0, :], MX[:, 0, :], -1.0, None, ALU.mult))
                sinks = SINK[:, 8:12] if sample else SINK[:, 4 * half:4 * half + 4]
                dve.tensor_tensor(DS[:, :], sinks, NM[:, 0, :], ALU.add).then_inc(sa_max, 1)

            def a_output(n):
                dve.wait_ge(sa_exp, n + 1)
                link(dve.tensor_tensor(SUM[:, 0, :], SUM[:, 0, :], ES[:, :], ALU.add))
                link(dve.reciprocal(RD[:, 0, :], SUM[:, 0, :]))
                dve.wait_ge(oa_mm, n + 1)
                o = PS[:, 4, 0:256].rearrange("p (c f) -> p c f", c=4)
                half = n % 2
                if n < N_JOBS_A - 1:
                    dve.tensor_tensor(OTA[:, :, half * HD:half * HD + HD], o,
                                      RD[:, 0, :].unsqueeze(2).to_broadcast([P, 4, HD]), ALU.mult).then_inc(oa_evac, 1)
                else:
                    for h in range(2):
                        ins = dve.tensor_tensor(OTA[:, 0:2, h * HD:h * HD + HD], o[:, 2 * h:2 * h + 2, :],
                                                RD[:, 0, 2 * h:2 * h + 2].unsqueeze(2).to_broadcast([P, 2, HD]), ALU.mult)
                    ins.then_inc(oa_evac, 1)

            for s in range(4):
                for g in range(3):
                    for j in range(4):
                        u = 12 * s + 4 * g + j
                        if u == 12:
                            dve.wait_ge(states_in, 16 * 8)
                            dve.wait_ge(x_split, 3)
                            link(dve.memset(CB[:, 0:2], 0.0))
                        ein_evac(4 * s + j, g, u)
                        if g == 2:
                            w_high(4 * s + j + NSLOT)
                        if u == 1:
                            w_high(3)
                            split_low(0, X, (1,))
                        if u == 3:
                            split_low(0, X, (2,))
                        if u == 23:
                            dve.wait_ge(p_evac, 24)
                            dve.tensor_copy(QS[:, :, :, :], Y[:, 0:4, SEQ:NT].rearrange("p c (b i) -> p b c i", b=DEC_BATCH))\
                               .then_inc(qs_ready, 1)
                        if s >= 2:
                            v = u - 24
                            if v % 2 == 0:
                                if v:
                                    a_output(v // 2 - 1)
                                a_scores(v // 2)
            for g in range(3):
                for j in range(2):
                    u = 48 + 2 * g + j
                    ein_evac(16 + j, g, u)
                    if g == 2:
                        w_high(16 + j + NSLOT)
                    v = u - 24
                    if v % 2 == 0:
                        a_output(v // 2 - 1)
                        a_scores(v // 2)
            for n in range(15, N_JOBS_A):
                a_output(n - 1)
                a_scores(n)
            a_output(N_JOBS_A - 1)
            split_low(1, Y)

            def out_super(l, s):
                base = U_EOUT if l == 0 else U_OOUT
                for g, (c0, gw) in enumerate(GROUP):
                    for j in range(4):
                        u = base + 12 * s + 4 * g + j
                        m = 4 * s + j
                        if s == 0 and j == 0:
                            dve.wait_ge(xr_in[l][g], 16)
                            if l == 0:
                                link(dve.tensor_scalar(X[:, :, c0:c0 + gw], X[:, :, c0:c0 + gw], ALPHA, None, ALU.mult))
                        dve.wait_ge(p_mm, u + 1)
                        bias = col((C_EBOUT if l == 0 else C_OBOUT) + m)
                        dve.scalar_tensor_tensor(out=X[:, m, c0:c0 + gw], in0=taken(u)[:, 0:gw], scalar=bias,
                                                 in1=X[:, m, c0:c0 + gw], op0=ALU.add, op1=ALU.add).then_inc(p_evac, 1)
                        if g == 2:
                            w_high((T_EOUT if l == 0 else T_OOUT) + m + NSLOT)
                        if s == 1:
                            ln_weave(2 * l, g, j)

            def hidden_low(l, i, weave):
                for g, (c0, gw) in enumerate(GROUP):
                    for j in range(4):
                        u = 4 * g + j
                        dve.wait_ge(hid_hi, 12 * i + (H_UNITS * l + u + 1))
                        dve.tensor_tensor(HID[:, 1, j, c0:c0 + gw], ST[:, u % 2, 0:gw],
                                          HID[:, 0, j, c0:c0 + gw].bitcast(F32), ALU.subtract).then_inc(hid_ready, 1)
                        if g == 2:
                            if weave is not None:
                                w_high(T_MLP[l] + j + NSLOT)
                            else:
                                w_high_loop(i, T_MLP[l] + j + NSLOT)
                        if weave is not None and g < 2:
                            ln_weave(weave, 3 + g, j)

            def down_super(l, i, weave):
                for g, (c0, gw) in enumerate(GROUP):
                    for m in range(8):
                        v = 8 * g + m
                        dve.wait_ge(p_mm, 24 * i + (U_MLP[l] + v + 1))
                        dve.tensor_tensor(X[:, m, c0:c0 + gw], X[:, m, c0:c0 + gw], taken(v)[:, 0:gw],
                                          ALU.add).then_inc(p_evac, 1)
                        if g == 2 and m % 2 == 1:
                            if weave is None:
                                w_high_loop(i, T_MLP[l] + m // 2 + 2 * NSLOT)
                            elif l == 0:
                                w_high(T_OIN + m // 2)
                        if weave is not None and m % 2 == 1:
                            ln_weave(weave, g, m // 2)

            def mlp(l):
                hidden_low(l, 0, 2 * l)
                dve.wait_ge(x_scaled, 48 * l + 24)
                with dve.Fori(0, N_HB - 1) as i:
                    down_super(l, i, None)
                    hidden_low(l, i + 1, None)
                down_super(l, N_HB - 1, 2 * l + 1)

            for s in range(2):
                out_super(0, s)
            mlp(0)

            def oin_evac(s, g, j, u):
                c0, gw = GROUP[g]
                ps = taken(u)[:, 0:gw]
                bias = col(C_OBIN + 4 * s + j)
                dve.wait_ge(p_mm, u + 1)
                if s == 0:
                    dve.tensor_scalar(Y[:, 4 + j, c0:c0 + gw], ps, bias, QSCALE, ALU.add, ALU.mult).then_inc(p_evac, 1)
                elif s == 1:
                    if g == 2:
                        dve.tensor_scalar(US[:, j, :, POOL_HIST:],
                                          ps[:, gw - NS:gw].rearrange("p (b i) -> p b i", b=DEC_BATCH), bias, None, ALU.add)
                        gw -= NS
                    dve.tensor_scalar(Y[:, j, c0:c0 + gw], ps[:, 0:gw], bias, None, ALU.add).then_inc(p_evac, 1)
                elif s == 2:
                    if g == 0 and j == 0:
                        dve.wait_ge(spilled, 48)
                    dve.tensor_scalar(KTD[:, j, c0:c0 + gw], ps, bias, None, ALU.add).then_inc(p_evac, 1)
                else:
                    dve.tensor_scalar(VT1[:, (4 * g + j) % 2, 0:gw], ps, bias, None, ALU.add).then_inc(p_evac, 1)

            def pooled(c):
                w = POOL_WINDOWS[c]
                if c:
                    dve.wait_ge(p_mm, U_OIN + 32 + 7 * c)
                u, src, dst, step = Y[:, c, 0:SEQ], PA, PB, 2
                dve.tensor_copy(UO[:, c, :], Y[:, c, SEQ - POOL_HIST:SEQ]).then_inc(uo_ready, 1)
                dve.tensor_copy(PA[:, 16:17], u[:, 0:1])
                link(dve.tensor_tensor(PA[:, 17:16 + SEQ], u[:, 1:SEQ], u[:, 0:SEQ - 1], ALU.add))
                while step < w:
                    link(dve.tensor_tensor(dst[:, 16:16 + SEQ], src[:, 16:16 + SEQ], src[:, 16 - step:16 - step + SEQ], ALU.add))
                    src, dst, step = dst, src, 2 * step
                link(dve.scalar_tensor_tensor(out=PO[:, 0:SEQ], in0=src[:, 16:16 + SEQ], scalar=1.0 / w, in1=u,
                                              op0=ALU.mult, op1=ALU.subtract))
                link(dve.tensor_tensor(PO[:, 0:16], src[:, 16:32], RC[:, c, :], ALU.mult))
                link(dve.tensor_tensor(PO[:, 0:16], PO[:, 0:16], u[:, 0:16], ALU.subtract))
                us, src, dst, step, lo = US[:, c, :, :], SA, SB, 2, 1
                link(dve.tensor_tensor(SA[:, :, 1:], us[:, :, 1:], us[:, :, :-1], ALU.add))
                while step < w:
                    lo += step
                    link(dve.tensor_tensor(dst[:, :, lo:], src[:, :, lo:], src[:, :, lo - step:23 - step], ALU.add))
                    src, dst, step = dst, src, 2 * step
                dve.scalar_tensor_tensor(out=PO[:, SEQ:NT].rearrange("p (b i) -> p b i", b=DEC_BATCH),
                                         in0=src[:, :, POOL_HIST:], scalar=1.0 / w, in1=us[:, :, POOL_HIST:],
                                         op0=ALU.mult, op1=ALU.subtract).then_inc(po_ready, 1)

            def group_evac(c, u0):
                for g, (c0, gw) in enumerate(GROUP):
                    dve.wait_ge(p_mm, u0 + g + 1)
                    dve.tensor_scalar(Y[:, c, c0:c0 + gw], taken(u0 + g)[:, 0:gw], col(C_CSCALE + c), None, ALU.mult)\
                       .then_inc(p_evac, 1)

            for s in range(3):
                for g in range(3):
                    for j in range(4):
                        oin_evac(s, g, j, U_OIN + 12 * s + 4 * g + j)
                        if g == 2:
                            w_high(T_OIN + 4 * s + j + NSLOT)
                        if s == 0 and g < 2:
                            ln_weave(1, 3 + g, j)
                        if s == 2 and g == 0 and j == 1:
                            dve.memset(PA[:, 0:16], 0.0)
                            link(dve.memset(PB[:, 0:16], 0.0))
                            pooled(0)
            group_evac(0, U_OIN + 36)
            for g in range(3):
                for j in range(4):
                    oin_evac(3, g, j, U_OIN + 39 + 7 * g + j)
                    if g == 2:
                        w_high(T_OOUT + j)
                    if j == 1:
                        pooled(g + 1)
                group_evac(g + 1, U_OIN + 39 + 7 * g + 4)

            def d_scores(m):
                h, qb = job_d(m)
                w = P * (qb + 1)
                if m % PER_SEQ == 0:
                    dve.wait_ge(th_in[h % 2], 16 * (h // 2 + 1))
                if m >= 3:
                    dve.wait_ge(ptd_mm, piece_base[m - 2])
                dve.wait_ge(sd_mm, m + 1)
                s = PS[:, scores_bank(m):scores_bank(m) + 2, :].rearrange("p a b -> p (a b)")
                link(dve.tensor_tensor_reduce(out=SMD[:, m % 3, 0:w], in0=s[:, 0:w], in1=TH[:, h % 2, SEQ - w:SEQ],
                                              scale=1.0, scalar=NEG, op0=ALU.add, op1=ALU.max,
                                              accum_out=MX[:, m % 2, 0:1]))
                dve.tensor_scalar(NM[:, m % 2, 0:1], MX[:, m % 2, 0:1], -1.0, None, ALU.mult).then_inc(sd_max, 1)

            def d_norm(m):
                w = P * (job_d(m)[1] + 1)
                dve.wait_ge(sd_exp, m + 1)
                link(dve.reciprocal(RD[:, m % 2, 0:1], SUM[:, m % 2, 0:1]))
                dve.tensor_scalar(SMD[:, m % 3, 0:w], SMD[:, m % 3, 0:w], RD[:, m % 2, 0:1], None,
                                  ALU.mult).then_inc(sd_prob, 1)

            def d_output(m):
                h, qb = job_d(m)
                lo = (h % 2) * HD
                dve.wait_ge(od_mm, m + 1)
                dve.tensor_copy(Y[lo:lo + HD, 4 + h // 2, qb * P:qb * P + P], PS[lo:lo + HD, 5, 0:P]).then_inc(od_evac, 1)

            def s_take(b, p):
                if p < 12:
                    e, c = divmod(p, 4)
                    n = 12 * b + p
                    nb = PIECES_S[e]
                    dve.wait_ge(ktc_mm, n + 1)
                    dve.tensor_copy(KTC[:, n % 4, 0:nb * P], bank(keys_bank(n), nb * P)).then_inc(ktc_evac, 1)
                if p and p % 4 == 0:
                    s_scores(b, p // 4 - 1)

            def s_scores(b, e):
                k0, k1 = 512 * e, min(512 * e + 512, KEYS_D)
                if e == 2:
                    link(dve.tensor_copy(BS[:, NB_D * P:], BNEW[:, b, :]))
                dve.wait_ge(ss_mm, 3 * b + e + 1)
                dve.tensor_tensor_reduce(out=SMS[:, k0:k1], in0=bank(6, k1 - k0), in1=BS[:, k0:k1], scale=1.0,
                                         scalar=MXS[:, e - 1:e] if e else NEG, op0=ALU.add, op1=ALU.max,
                                         accum_out=MXS[:, e:e + 1]).then_inc(ss_taken, 1)
                dve.wait_ge(ss_taken, 3 * b + e + 1)
                if e == 2:
                    dve.tensor_scalar(NM[:, 0, 1:2], MXS[:, 2:3], -1.0, None, ALU.mult).then_inc(ss_max, 1)

            def s_scale(b):
                dve.wait_ge(ss_exp, b + 1)
                link(dve.reciprocal(RD[:, 0, 1:2], SUM[:, 0, 1:2]))
                dve.wait_ge(os_mm, b + 1)
                dve.tensor_scalar(OS[:, :], PS[:, 5, P:2 * P], RD[:, 0, 1:2], None, ALU.mult).then_inc(os_scaled, 1)

            def s_output(b):
                dve.wait_ge(ost_mm, b + 1)
                o = PS[:, 5, P:2 * P].rearrange("p (c r) -> p c r", c=4)
                dve.tensor_copy(Y[0:HD, 4:8, SEQ + 8 * b:SEQ + 8 * b + 8], o[0:HD, :, 0:DEC_SEQ])
                dve.tensor_copy(Y[HD:P, 4:8, SEQ + 8 * b:SEQ + 8 * b + 8], o[HD:P, :, DEC_SEQ:2 * DEC_SEQ]).then_inc(os_evac, 1)

            dve.memset(QBD[:, :, :, :], 0.0).then_inc(qbd_zero, 1)
            d_scores(0)
            d_scores(1)
            d_norm(0)
            dve.wait_ge(bs_in, 32)
            dve.wait_ge(w_split, T_OOUT + 4)
            for m in range(JOBS_D):
                b, step = divmod(m, PER_SEQ)
                if m:
                    d_output(m - 1)
                if step < 6:
                    s_take(b, 2 * step)
                if m + 1 < JOBS_D:
                    d_norm(m + 1)
                if step == 6:
                    s_take(b, 12)
                if step == 4 and b:
                    s_scale(b - 1)
                if step == 5 and b:
                    s_output(b - 1)
                if m + 2 < JOBS_D:
                    d_scores(m + 2)
                if step < 6:
                    s_take(b, 2 * step + 1)
            d_output(JOBS_D - 1)
            s_scale(DEC_BATCH - 1)
            s_output(DEC_BATCH - 1)
            split_low(2, Y)
            for s in range(2):
                out_super(1, s)
            mlp(1)
            for j in range(1, 4):
                ln_weave(3, 3, j)
            c0, gw = GROUP[2]
            for k in range(1, KC, 2):
                dve.wait_ge(bt_mm, 88 + k + 1)
                dve.tensor_scalar(X[:, k, c0:c0 + gw], bank(back_bank(3, 2, k), gw), col(C_LNG + KC * 3 + k),
                                  col(C_LNB + KC * 3 + k), ALU.mult, ALU.add).then_inc(b_evac_odd, 1)

        @block.tensor
        def _(pe):
            def product(out, slot, off, nk, src, g, done):
                c0, gw = GROUP[g]
                n = 0
                for k in range(nk):
                    for a, b in ((0, 0), (1, 0), (0, 1)):
                        last = pe.matmul(out[:, 0:gw], WS[:, slot, a, (off + k) * P:(off + k + 1) * P],
                                         src[:, b, k, c0:c0 + gw], start=(n == 0), stop=(n == 3 * nk - 1))
                        n += 1
                last.then_inc(done, 1)

            def unit(u, t, g):
                if g == 0:
                    pe.wait_ge(w_split, t + 1)
                if u >= 2:
                    pe.wait_ge(p_evac, u - 1)
                product(bank(6 + u % 2), t % NSLOT, 0, KC, XS, g, p_mm)

            def ln_weave(l, phase, quarter, group_done, parts="BF"):
                if "B" in parts and 0 <= phase - 2 <= 2 and quarter < 3:
                    g = phase - 2
                    for k in BACK_CHUNKS[quarter]:
                        n = 24 * l + 8 * g + k
                        if k == 0:
                            pe.wait_ge(zn_ready, 9 * l + 3 * g + 3)
                        if (l, g) == (3, 2) and k >= 4:
                            pe.wait_ge(b_evac_odd if k % 2 else b_evac, (k - 3) // 2 if k % 2 else 88 + k // 2 - 1)
                        elif (l, g) == (3, 2):
                            pe.wait_ge(b_evac, 88)
                        elif n >= 2:
                            pe.wait_ge(b_evac, n - 1)
                        for tt in range(3):
                            r = tile_rows(3 * g + tt)
                            last = pe.transpose(PS[:, back_bank(l, g, k), tt * P:tt * P + r],
                                                rows_out(l, g)[0:r, tt, k * P:k * P + P],
                                                IDN[0:r, 0:r])
                        last.then_inc(bt_mm, 1)
                if "F" in parts and 0 <= phase - 1 <= 2 and quarter > 0:
                    g, tt = phase - 1, quarter - 1
                    t = 3 * g + tt
                    r = tile_rows(t)
                    if tt == 0:
                        pe.wait_ge(p_evac, group_done[g])
                    if t >= 2:
                        pe.wait_ge(zn_ready, 9 * l + t - 1)
                    elif t == 0 and l % 2:
                        pe.wait_ge(h_evac, H_UNITS * (l + 1) // 2)
                    FT = rows_in(l, t)
                    for k in range(KC):
                        last = pe.transpose(FT[0:r, k * P:k * P + P], X[:, k, t * P:t * P + r], IDN[:, :])
                    last.then_inc(ft_mm, 1)

            def v_transpose(n, src, gw):
                if n >= 2:
                    pe.wait_ge(vt_evac, n - 1)
                for tt in range(3):
                    r = min(P, gw - tt * P)
                    last = pe.transpose(PS[0:r, 4 + n % 2, tt * P:tt * P + P], src[:, tt * P:tt * P + r], IDN[:, :])
                last.then_inc(vt_mm, 1)

            pe.wait_ge(ident_in, 16)
            for s in range(2):
                for g in range(3):
                    if s == 0:
                        pe.wait_ge(x_split, g + 1)
                    for j in range(4):
                        unit(12 * s + 4 * g + j, 4 * s + j, g)
                        if s == 0 and j == 2:
                            pe.wait_ge(p_evac, 4 * g + 2)
                            v_transpose(g, VT0[:, g % 2, :], GROUP[g][1])
            pe.wait_ge(vt_evac, 3)
            pe.transpose(PS[0:NS, 4, 0:P], KTA[:, SEQ:NT], IDN[:, :]).then_inc(kn_mm, 1)
            pe.wait_ge(kca_in, 16)
            for h in range(2):
                for b in range(4):
                    last = pe.transpose(PS[:, 2 + h, b * P:b * P + P], KCA[:, 4 * h + b, :], IDN[:, :])
                last.then_inc(kct_mm, 1)

            def a_scores(n):
                w, nk, k0 = job_a(n)
                qb, half = divmod(n, 2)
                lo = half * HD
                if n:
                    pe.wait_ge(sa_max, n)
                else:
                    pe.wait_ge(p_evac, 24)
                s = PS[:, 0:2, :].rearrange("p a (b f) -> p (a b) f", f=256)
                if n < N_JOBS_A - 1:
                    for c in range(4):
                        last = pe.matmul(s[:, c, 0:w], Y[lo:lo + HD, c, qb * P:qb * P + P],
                                         KTA[lo:lo + HD, k0:k0 + w], start=True, stop=True)
                else:
                    pe.wait_ge(kct_evac, 2)
                    pe.wait_ge(qs_ready, 1)
                    for half in range(2):
                        lo = half * HD
                        for b in range(DEC_BATCH):
                            rows = 32 * (b % 4)
                            q = QS[lo:lo + HD, b, :, :].rearrange("p c i -> p (c i)")
                            o = s[rows:rows + 32, 2 * half + b // 4, :]
                            pe.matmul(o[:, 0:P], q, KCT[lo:lo + HD, b, :], start=True, stop=True)
                            last = pe.matmul(o[:, P:192], q, KTA[lo:lo + HD, SEQ:NT], start=True, stop=True)
                last.then_inc(sa_mm, 1)

            def a_transpose(n):
                w, nk, k0 = job_a(n)
                pe.wait_ge(sa_exp, n + 1)
                if n:
                    pe.wait_ge(pta_evac, n)
                o = PS[:, 2:4, :].rearrange("p a (b f) -> p (a b) f", f=P)
                if n < N_JOBS_A - 1:
                    for c in range(4):
                        for kb in range(nk):
                            last = pe.transpose(o[:, nk * c + kb, :], SMA[:, c, kb * P:kb * P + P], IDN[:, :])
                else:
                    for i in range(4):
                        pe.transpose(o[:, i, :], SMA[:, i, 0:P], IDN[:, :])
                        last = pe.transpose(o[0:NS, 4 + i, :], SMA[:, i, P:192], IDN[:, :])
                last.then_inc(pta_mm, 1)

            def a_values(n):
                w, nk, k0 = job_a(n)
                qb, half = divmod(n, 2)
                pe.wait_ge(pta_evac, n + 1)
                if n:
                    pe.wait_ge(oa_evac, n)
                else:
                    pe.wait_ge(kn_evac, 1)
                o = PS[:, 4, 0:256].rearrange("p (c f) -> p c f", c=4)
                if n < N_JOBS_A - 1:
                    for c in range(4):
                        for kb in range(nk):
                            last = pe.matmul(o[:, c, :], PTA[:, nk * c + kb, :],
                                             VA[:, k0 // P + kb, half * HD:half * HD + HD],
                                             start=(kb == 0), stop=(kb == nk - 1))
                else:
                    pe.wait_ge(vca_in, 16)
                    for half in range(2):
                        hd = slice(half * HD, half * HD + HD)
                        for b in range(DEC_BATCH):
                            rows = slice(32 * (b % 4), 32 * (b % 4) + 32)
                            i = 2 * half + b // 4
                            pe.matmul(o[rows, i, :], PTA[:, i, rows], VCA[:, b, hd], start=True, stop=False)
                            last = pe.matmul(o[rows, i, :], PTA[0:NS, 4 + i, rows], VA[0:NS, 8, hd],
                                             start=False, stop=True)
                last.then_inc(oa_mm, 1)

            def a_out(qb):
                pe.wait_ge(oa_evac, 2 * qb + 2)
                if qb:
                    pe.wait_ge(ota_evac, qb)
                for c in range(4):
                    last = pe.transpose(PS[:, 5, c * P:c * P + P], OTA[:, c, :], IDN[:, :])
                last.then_inc(ota_mm, 1)

            def a_slot(v):
                n = v // 2
                if v % 2 == 0:
                    if n:
                        a_values(n - 1)
                    a_scores(n)
                else:
                    a_transpose(n)
                    if n >= 2 and n % 2 == 0:
                        a_out(n // 2 - 1)

            for s in range(2, 4):
                for g in range(3):
                    for j in range(4):
                        unit(12 * s + 4 * g + j, 4 * s + j, g)
                        a_slot(12 * (s - 2) + 4 * g + j)
            for g in range(3):
                for j in range(2):
                    unit(48 + 2 * g + j, 16 + j, g)
                    a_slot(24 + 2 * g + j)
            for n in range(15, N_JOBS_A):
                a_slot(2 * n)
                a_slot(2 * n + 1)
            a_values(N_JOBS_A - 1)
            pe.wait_ge(oa_evac, N_JOBS_A)
            pe.wait_ge(ota_evac, 8)
            for quad in range(2):
                last = pe.transpose(PS[:, 5, quad * P:quad * P + P], OTA[:, quad, :], IDN[:, :])
            last.then_inc(ota_mm, 1)

            def out_projection(l, t0, u0, xs):
                done = [u0 + 12 + 4 * g + 4 for g in range(3)]
                for s in range(2):
                    for g in range(3):
                        if s == 0:
                            pe.wait_ge(x_split, xs + g + 1)
                        for j in range(4):
                            unit(u0 + 12 * s + 4 * g + j, t0 + 4 * s + j, g)
                            if s == 1:
                                ln_weave(2 * l, g, j, done)
                return done

            def hidden_super(l, i, weave, done):
                t0 = T_MLP[l]
                for g in range(3):
                    if weave is not None:
                        pe.wait_ge(x_split, XS_LN[2 * l] + 8 * (g + 1))
                        if g == 0:
                            pe.wait_ge(zn_ready, 18 * l + 5)
                    for j in range(4):
                        u = 4 * g + j
                        n = 12 * i + (H_UNITS * l + u)
                        if g == 0:
                            pe.wait_ge(w_split, 8 * i + (t0 + j + 1))
                        if not (isinstance(n, int) and n < 2):
                            pe.wait_ge(h_evac, n - 1)
                        product(bank(4 + u % 2), (t0 + j) % NSLOT, 0, KC, XS, g, h_mm)
                        if weave is not None and g < 2:
                            ln_weave(weave, 3 + g, j, done)

            def down_super(l, i, weave):
                t0 = T_MLP[l] + 4
                done = [U_MLP[l] + 24 * (N_HB - 1) + 8 * g + 8 for g in range(3)]
                for g in range(3):
                    pe.wait_ge(hid_ready, 12 * i + (H_UNITS * l + 4 * g + 4))
                    for j in range(4):
                        if g == 0:
                            pe.wait_ge(w_split, 8 * i + (t0 + j + 1))
                        for mm in range(2):
                            v = 8 * g + 2 * j + mm
                            pe.wait_ge(p_evac, 24 * i + (U_MLP[l] + v - 1))
                            product(bank(6 + v % 2), (t0 + j) % NSLOT, 4 * mm, 4, HID, g, p_mm)
                        if weave is not None:
                            ln_weave(weave, g, j, done)
                return done

            def mlp(l, done):
                hidden_super(l, 0, 2 * l, done)
                with pe.Fori(0, N_HB - 1) as i:
                    down_super(l, i, None)
                    hidden_super(l, i + 1, None, None)
                return down_super(l, N_HB - 1, 2 * l + 1)

            pe.wait_ge(ota_evac, 10)
            done = mlp(0, out_projection(0, T_EOUT, U_EOUT, XS_MIX0))

            def group_product(c, u0):
                pe.wait_ge(po_ready, c + 1)
                for g, (c0, gw) in enumerate(GROUP):
                    pe.wait_ge(p_evac, u0 + g - 1)
                    pe.matmul(bank(6 + (u0 + g) % 2, gw), GW[:, c, :], PO[:, c0:c0 + gw],
                              start=True, stop=True).then_inc(p_mm, 1)

            for s in range(4):
                for g in range(3):
                    if s == 0:
                        pe.wait_ge(x_split, XS_LN1 + 8 * (g + 1))
                    for j in range(4):
                        n = 4 * g + j
                        unit(U_OIN + (12 * s + 4 * g if s < 3 else 39 + 7 * g) + j, T_OIN + 4 * s + j, g)
                        if s == 0 and g < 2:
                            ln_weave(1, 3 + g, j, done)
                        if s == 3 and n:
                            pg, pj = divmod(n - 1, 4)
                            pe.wait_ge(p_evac, U_OIN + 39 + 7 * pg + pj + 1)
                            v_transpose(3 + n - 1, VT1[:, (n - 1) % 2, :], GROUP[pg][1])
                    if s == 3:
                        if g == 2:
                            pe.wait_ge(p_evac, U_OIN + 57)
                            v_transpose(14, VT1[:, 1, :], GROUP[2][1])
                        group_product(g + 1, U_OIN + 39 + 7 * g + 4)
                if s == 2:
                    pe.wait_ge(p_evac, U_OIN + 36)
                    pe.wait_ge(b_evac, 48)
                    for c in range(4):
                        last = pe.transpose(PS[0:NS, 3, c * P:c * P + P], KTD[:, c, SEQ:NT], IDN[:, :])
                    last.then_inc(kn_mm, 1)
                    group_product(0, U_OIN + 36)

            def d_scores(m):
                h, qb = job_d(m)
                w = P * (qb + 1)
                pe.wait_ge(qp_ready, m + 1)
                if m >= 2:
                    pe.wait_ge(sd_max, m - 1)
                for k0 in range(0, w, 512):
                    kw = min(512, w - k0)
                    last = pe.matmul(bank(scores_bank(m) + k0 // 512, kw), QP[:, h % 2, m % 2, :],
                                     KTD[:, h // 2, k0:k0 + kw], start=True, stop=True)
                last.then_inc(sd_mm, 1)

            def d_transpose(m, part):
                pe.wait_ge(sd_prob, m + 1)
                for e, (k, nk) in enumerate(pieces_d(m)):
                    if e != part:
                        continue
                    n = piece_base[m] + e
                    if n:
                        pe.wait_ge(ptd_evac, n)
                    for kb in range(nk):
                        last = pe.transpose(PS[:, 4, kb * P:kb * P + P], SMD[:, m % 3, (k + kb) * P:(k + kb + 1) * P],
                                            IDN[:, :])
                    last.then_inc(ptd_mm, 1)

            def d_values(m):
                h, qb = job_d(m)
                pe.wait_ge(ptd_evac, piece_base[m] + len(pieces_d(m)))
                if m:
                    pe.wait_ge(od_evac, m)
                if m % PER_SEQ == 4 and m > PER_SEQ:
                    pe.wait_ge(os_scaled, m // PER_SEQ)
                if m % PER_SEQ == 5 and m > PER_SEQ:
                    pe.wait_ge(os_evac, m // PER_SEQ)
                lo = (h % 2) * HD
                for kb in range(qb + 1):
                    last = pe.matmul(PS[lo:lo + HD, 5, 0:P], VD[:, kb, h * HD:h * HD + HD], PTD[:, m % 2, kb, :],
                                     start=(kb == 0), stop=(kb == qb))
                last.then_inc(od_mm, 1)

            def s_keys(b, p):
                e, c = divmod(p, 4)
                if c == 0:
                    pe.wait_ge(ks_in[e], (64 if e == 2 else 16) * (b + 1))
                if b and p < 2:
                    pe.wait_ge(pts_evac, 3 * b - 2 + p)
                if 12 * b + p >= 2:
                    pe.wait_ge(ktc_evac, 12 * b + p - 1)
                for i in range(PIECES_S[e]):
                    last = pe.transpose(PS[:, keys_bank(12 * b + p), i * P:i * P + P], KCD[:, 4 * e + i, c * P:c * P + P], IDN[:, :])
                last.then_inc(ktc_mm, 1)

            def s_scores(b, p):
                e, c = divmod(p, 4)
                n = 12 * b + p
                pe.wait_ge(ktc_evac, n + 1)
                if p == 0:
                    pe.wait_ge(qbd_ready, b + 1)
                if c == 0 and 3 * b + e:
                    pe.wait_ge(ss_taken, 3 * b + e)
                if p == 0 and b:
                    pe.wait_ge(pts_evac, 3 * b)
                rows = slice(32 * c, 32 * c + 32)
                kw = PIECES_S[e] * P
                last = pe.matmul(PS[rows, 6, 0:kw], QBD[:, b % 2, c, :], KTC[:, n % 4, 0:kw], start=True, stop=True)
                if e == 2:
                    last = pe.matmul(PS[rows, 6, kw:kw + NS], QBD[:, b % 2, c, :], KTD[:, c, SEQ:NT], start=True, stop=True)
                if c == 3:
                    last.then_inc(ss_mm, 1)

            def s_step(b, p):
                if p < 12:
                    s_keys(b, p)
                if p:
                    s_scores(b, p - 1)

            def s_transpose(b, e):
                if e == 0:
                    pe.wait_ge(ss_exp, b + 1)
                pe.wait_ge(ktc_evac, 12 * b + 12)
                pe.wait_ge(ss_taken, 3 * b + 3)
                o = PT_BANK_S[e]
                for i in range(PIECES_S[e]):
                    last = pe.transpose(PS[:, o, i * P:i * P + P], SMS[:, (4 * e + i) * P:(4 * e + i + 1) * P],
                                        IDN[:, :])
                if e == 2:
                    last = pe.transpose(PS[0:NS, o, 2 * P:3 * P], SMS[:, NB_D * P:], IDN[:, :])
                last.then_inc(pts_mm, 1)

            def s_values(b, c):
                if c == 0:
                    pe.wait_ge(pts_evac, 3 * b + 3)
                    pe.wait_ge(vs_in, 96 * (b + 1))
                pe.wait_ge(od_evac, min(JOBS_D, PER_SEQ * (b + 1) + 1 + c))
                rows = slice(32 * c, 32 * c + 32)
                for i in range(NB_D):
                    pe.matmul(PS[rows, 5, P:2 * P], PTS[:, i, rows], VCD[:, i, c * P:c * P + P], start=(i == 0), stop=False)
                last = pe.matmul(PS[rows, 5, P:2 * P], PTS[0:NS, NB_D, rows], VN[:, c * P:c * P + P], start=False, stop=True)
                if c == 3:
                    last.then_inc(os_mm, 1)

            def s_output(b):
                pe.wait_ge(os_scaled, b + 1)
                pe.wait_ge(od_evac, min(JOBS_D, PER_SEQ * (b + 1) + 5))
                pe.transpose(PS[:, 5, P:2 * P], OS[:, :], IDN[:, :]).then_inc(ost_mm, 1)

            pe.wait_ge(p_evac, U_OOUT)
            pe.wait_ge(kn_evac, 2)
            pe.wait_ge(vt_evac, 15)
            d_scores(0)
            d_scores(1)
            for m in range(JOBS_D):
                b, step = divmod(m, PER_SEQ)
                d_transpose(m, 0)
                if m:
                    d_values(m - 1)
                if step == 0 and b:
                    s_transpose(b - 1, 2)
                if step <= 6:
                    s_step(b, 2 * step)
                if 1 <= step <= 4 and b:
                    s_values(b - 1, step - 1)
                elif step == 5 and b:
                    s_output(b - 1)
                d_transpose(m, 1)
                if m + 2 < JOBS_D:
                    d_scores(m + 2)
                if step < 6:
                    s_step(b, 2 * step + 1)
                elif step == 7:
                    s_transpose(b, 0)
                    s_transpose(b, 1)
            d_values(JOBS_D - 1)
            s_transpose(DEC_BATCH - 1, 2)
            for c in range(4):
                s_values(DEC_BATCH - 1, c)
            s_output(DEC_BATCH - 1)
            pe.wait_ge(os_evac, DEC_BATCH)
            done = mlp(1, out_projection(1, T_OOUT, U_OOUT, XS_MIX1))
            for j, part in ((1, "F"), (2, "F"), (0, "B"), (1, "B"), (3, "F"), (2, "B")):
                ln_weave(3, 3, j, done, part)
            for j in range(3):
                ln_weave(3, 4, j, done, "B")


def slopes(n):
    return 2.0 ** (-8.0 * np.arange(1, n + 1) / n)


def dilated(dist):
    n = sum(((dist >= 0) & (dist <= w) & (dist % d == 0)).astype(np.float64) for w, d in D_BRANCHES)
    return np.where(n > 0, np.log(np.maximum(n, 1)), NEG)


def tables():
    p = np.arange(P)
    sl = slopes(A_HEADS)
    t = {"ident": np.eye(P)}
    dist = P + p[:, None] - np.arange(2 * P)[None, :]
    ok = (dist >= 0) & (dist <= A_WINDOW)
    t["ba"] = np.stack([np.stack([np.where(ok, -sl[4 * half + c] * dist, NEG) for c in range(4)], 1)
                        for half in range(2)], 1)
    bb, c, i = p // 32, p % 32 // 8, p % 8
    sets = []
    for half in range(2):
        s = sl[4 * half + c][:, None]
        for quad in range(2):
            dist = A_WINDOW + i[:, None] - p[None, :]
            old = np.where((dist >= 0) & (dist <= A_WINDOW), -s * dist, NEG)
            nb, ni = np.arange(NS)[None, :] // 8, np.arange(NS)[None, :] % 8
            ok = (nb == 4 * quad + bb[:, None]) & (ni <= i[:, None])
            sets.append(np.concatenate([old, np.where(ok, -s * (i[:, None] - ni), NEG)], 1))
    t["bas"] = np.stack(sets, 1)
    dist = SEQ - P + p[:, None] - np.arange(SEQ)[None, :]
    t["th"] = np.stack([np.where(dist >= 0, -s * dist, 0) + dilated(dist) for s in slopes(D_HEADS)])
    c, hh, i = p // 32, p % 32 // 8, p % 8
    s = np.where(hh < 2, slopes(D_HEADS)[np.minimum(2 * c + hh, D_HEADS - 1)], 0)[:, None]
    live = (hh < 2)[:, None]
    rows = np.zeros((NB_D, P), int)
    for blk in range(8):
        rows[blk] = 16 * p + blk
    for e in range(2):
        rows[8 + e] = 16 * (96 + p % 32) + 8 + 2 * (p // 32) + e
    dist = D_WINDOW + i[:, None] - rows.reshape(-1)[None, :]
    t["bs"] = np.where(live, -s * dist + dilated(dist), 0)
    nb, ni = np.arange(NS)[None, :] // 8, np.arange(NS)[None, :] % 8
    d = i[:, None] - ni
    t["bnew"] = np.stack([np.where(live, np.where(nb == b, -s * d + dilated(d), NEG), 0) for b in range(DEC_BATCH)], 1)
    w = np.array(POOL_WINDOWS)[:, None]
    t["rc"] = np.broadcast_to(1.0 / np.minimum(np.arange(16)[None, :] + 1, w), (P, 4, 16))
    return {k: np.ascontiguousarray(v, dtype=np.float32) for k, v in t.items()}


def kernel(x_prompt, x_sample, cache_a_k, cache_a_v, state_b_conv, state_c_pool, cache_d_k, cache_d_v,
           even_w_in, even_b_in, a_sinks, b_conv_w, even_w_out, even_b_out,
           odd_w_in, odd_b_in, c_w_group, c_scale, odd_w_out, odd_b_out,
           mlp_w1, mlp_w2, ln1_g, ln1_b, ln2_g, ln2_b):
    import concourse.bacc as bacc
    from concourse.bass_utils import run_bass_kernel_spmd as run

    A = np.asarray
    B = DEC_BATCH

    def features(a):
        a = A(a).reshape(-1, a.shape[-1])
        return a.T.reshape(a.shape[1] // P, P, a.shape[0]).transpose(1, 0, 2)

    def in_tiles(w):
        w = A(w)
        n = w.shape[1] // P
        return w.reshape(KC, P, n, P).transpose(2, 1, 0, 3).reshape(n, P, 1024)

    def down_tiles(w):
        return A(w).reshape(4, P, 4, 2, P).transpose(2, 1, 3, 0, 4).reshape(4, P, 1024)

    pairs = np.arange(A_HEADS * HD).reshape(2, 4, HD).transpose(1, 0, 2).reshape(-1)
    e = np.arange(4 * P).reshape(4, P)
    order = np.concatenate([512 + np.arange(256), pairs] + [np.concatenate([768 + e[j], 1792 + e[j], 1280 + e[j]]) for j in range(4)])
    o = np.arange(512)
    oorder = np.concatenate([512 + o, o, 1024 + o, 1536 + o])
    w1, w2 = A(mlp_w1), A(mlp_w2)

    def mlp_tiles(l):
        return [t for h in range(N_HB) for t in (in_tiles(w1[l][:, 512 * h:512 * h + 512]),
                                                 down_tiles(w2[l][512 * h:512 * h + 512]))]

    w = np.concatenate([in_tiles(A(even_w_in)[0][:, order]),
                        in_tiles(A(even_w_out)[0][np.concatenate([pairs, 512 + o])])] + mlp_tiles(0)
                       + [in_tiles(A(odd_w_in)[0][:, oorder]), in_tiles(A(odd_w_out)[0])] + mlp_tiles(1))

    def columns(*vs):
        return [A(v).reshape(-1, P).T for v in vs]

    cols = np.concatenate(columns(A(even_b_in)[0][order], A(b_conv_w)[0], even_b_out, A(odd_b_in)[0][oorder], c_scale,
                                  odd_b_out, ln1_g[0], ln2_g[0], ln1_g[1], ln2_g[1],
                                  ln1_b[0], ln2_b[0], ln1_b[1], ln2_b[1]), 1)
    head = np.arange(P) % 32 // 8
    sinks = A(a_sinks)[0]
    sink = np.concatenate([np.broadcast_to(sinks, (P, 8)),
                           np.stack([sinks[head], sinks[head], sinks[head + 4], sinks[head + 4]], 1)], 1)
    ins = dict(tables())
    ins.update(
        x=np.concatenate([features(x_prompt), features(x_sample)], 2), w=w, cols=cols, sink=sink,
        gw=A(c_w_group)[0].transpose(1, 0, 2),
        b_state=features(state_b_conv).reshape(P, 4, B, 2), c_state=features(state_c_pool).reshape(P, 4, B, POOL_HIST),
        cache_a_k=A(cache_a_k).reshape(B, A_WINDOW, P), cache_a_v=A(cache_a_v).reshape(B, A_WINDOW, P),
        cache_d_k=A(cache_d_k).reshape(B, D_WINDOW, 512), cache_d_v=A(cache_d_v).reshape(B, D_WINDOW, 512))
    ins = {k: np.ascontiguousarray(v) for k, v in ins.items()}
    outs = dict(y=(P, KC, NT), a_k=(P, A_WINDOW), a_v=(A_WINDOW, P), b_c=(P, 4, 2), c_p=(P, 4, POOL_HIST),
                d_k=(P, 4, SEQ), d_v=(SEQ, 512), a_ks=(B, A_WINDOW, P), a_vs=(B, A_WINDOW, P),
                b_cs=(P, 4, B, 2), c_ps=(P, 4, B, POOL_HIST), d_ks=(B, D_WINDOW, 512), d_vs=(B, D_WINDOW, 512))

    nc = bacc.Bacc("TRN2", target_bir_lowering=False, num_devices=1)
    F32 = mybir.dt.float32
    io = {k: nc.dram_tensor("in_" + k, v.shape, F32, kind="ExternalInput").ap() for k, v in ins.items()}
    io.update({k: nc.dram_tensor("out_" + k, v, F32, kind="ExternalOutput").ap() for k, v in outs.items()})
    io["spill"] = nc.dram_tensor("spill", (P, KC, NT), F32, kind="Internal").ap()
    build(nc, io)
    r = run(nc, [{"in_" + k: v for k, v in ins.items()}], core_ids=[0]).results[0]
    r = {k: r["out_" + k] for k in outs}

    def tokens(a):
        return a.transpose(2, 1, 0).reshape(a.shape[2], -1)

    y = tokens(r["y"])
    return (y[:SEQ].reshape(1, SEQ, D_MODEL), y[SEQ:].reshape(B, DEC_SEQ, D_MODEL),
            r["a_k"].T.reshape(1, 1, A_WINDOW, 2, HD), r["a_v"].reshape(1, 1, A_WINDOW, 2, HD),
            tokens(r["b_c"]).reshape(1, 1, 2, B_WIDTH), tokens(r["c_p"]).reshape(1, 1, POOL_HIST, 512),
            tokens(r["d_k"]).reshape(1, 1, SEQ, 8, HD), r["d_v"].reshape(1, 1, SEQ, 8, HD),
            r["a_ks"].reshape(1, B, A_WINDOW, 2, HD), r["a_vs"].reshape(1, B, A_WINDOW, 2, HD),
            tokens(r["b_cs"].reshape(P, 4, B * 2)).reshape(1, B, 2, B_WIDTH),
            tokens(r["c_ps"].reshape(P, 4, B * POOL_HIST)).reshape(1, B, POOL_HIST, 512),
            r["d_ks"].reshape(1, B, D_WINDOW, 8, HD), r["d_vs"].reshape(1, B, D_WINDOW, 8, HD))
```
